# Optimizing a Trainium2 kernel written in Bass

```python
import math
import jax, jax.numpy as jnp
from jax import lax
import numpy as np

D_MODEL = 2048
BATCH = 1
SEQ = 256
DEPTH = 1

CHUNK = 64
Q_BLOCK = 128
HEAD_DIM = 128
D_MIX = D_MODEL
D_SB = D_MIX // 2
D_CH = D_MIX - D_SB
N_HEADS_SB = D_SB // HEAD_DIM
N_HEADS_CH = D_CH // HEAD_DIM
LEFT_CHUNKS = 8
BAND = LEFT_CHUNKS + 1
REL_CLIP = 256
N_REL = REL_CLIP + CHUNK
D_IN = 4 * D_SB + 4 * D_CH
NORM_EPS = 1e-6
NEG_BIG = -1e30


def rms_norm(x, g):
    xf = x.astype(jnp.float32)
    y = xf * lax.rsqrt(jnp.mean(xf * xf, axis=-1, keepdims=True) + NORM_EPS)
    return (y * g.astype(jnp.float32)).astype(x.dtype)

def split_heads(t, n_heads):
    b, s, _ = t.shape
    return t.reshape(b, s, n_heads, HEAD_DIM).transpose(0, 2, 1, 3)

def merge_heads(t):
    b, h, s, d = t.shape
    return t.transpose(0, 2, 1, 3).reshape(b, s, h * d)

def stick_breaking_attention(q, k, v):
    seq = q.shape[2]
    scale = q.shape[-1] ** -0.5
    outs = []
    for blk in range(seq // Q_BLOCK):
        t0 = blk * Q_BLOCK
        t1 = t0 + Q_BLOCK
        qb = q[:, :, t0:t1]
        kb = k[:, :, :t1]
        vb = v[:, :, :t1]
        z = jnp.einsum('bhtd,bhsd->bhts', qb, kb).astype(jnp.float32) * scale
        t_idx = jnp.arange(t0, t1)[:, None]
        s_idx = jnp.arange(t1)[None, :]
        causal = s_idx < t_idx
        log_stay = jnp.where(causal, jax.nn.log_sigmoid(-z), 0.0)
        after = lax.cumsum(log_stay, axis=3, reverse=True) - log_stay
        w = jnp.where(causal, jnp.exp(jax.nn.log_sigmoid(z) + after), 0.0)
        outs.append(jnp.einsum('bhts,bhsd->bhtd', w.astype(v.dtype), vb))
    return jnp.concatenate(outs, axis=2)

def chunk_band_attention(q, k, v, q_gain, k_gain, rel_table):
    b, h, seq, d = q.shape
    nc = seq // CHUNK
    q = rms_norm(q, q_gain)
    k = rms_norm(k, k_gain)
    qc = q.reshape(b, h, nc, CHUNK, d)
    pad = ((0, 0), (0, 0), (LEFT_CHUNKS * CHUNK, 0), (0, 0))
    kc = jnp.pad(k, pad).reshape(b, h, nc + LEFT_CHUNKS, CHUNK, d)
    vc = jnp.pad(v, pad).reshape(b, h, nc + LEFT_CHUNKS, CHUNK, d)
    band_idx = jnp.arange(nc)[:, None] + jnp.arange(BAND)[None, :]
    kband = kc[:, :, band_idx].reshape(b, h, nc, BAND * CHUNK, d)
    vband = vc[:, :, band_idx].reshape(b, h, nc, BAND * CHUNK, d)
    scores = jnp.einsum('bhcid,bhcpd->bhcip', qc, kband).astype(jnp.float32) * (d ** -0.5)
    i_pos = np.arange(CHUNK)[:, None]
    p_pos = np.arange(BAND * CHUNK)[None, :]
    dist = LEFT_CHUNKS * CHUNK + i_pos - p_pos
    rel_idx = np.clip(dist, -(CHUNK - 1), REL_CLIP) + (CHUNK - 1)
    bias = rel_table.astype(jnp.float32)[:, rel_idx]
    scores = scores + bias[None, :, None]
    valid = jnp.repeat(band_idx >= LEFT_CHUNKS, CHUNK, axis=1)
    scores = jnp.where(valid[None, None, :, None, :], scores, NEG_BIG)
    probs = jax.nn.softmax(scores, axis=-1)
    out = jnp.einsum('bhcip,bhcpd->bhcid', probs.astype(v.dtype), vband)
    return out.reshape(b, h, seq, d)

def first_inputs(seed: int = 0) -> dict:
    key = jax.random.key(seed)
    ks = jax.random.split(key, 8)
    x = jax.random.normal(ks[0], (BATCH, SEQ, D_MODEL), jnp.float32)
    norm_g = 1.0 + 0.02 * jax.random.normal(ks[1], (DEPTH, D_MODEL), jnp.float32)
    w_in = jax.random.normal(ks[2], (DEPTH, D_MODEL, D_IN), jnp.float32) * D_MODEL ** -0.5
    q_norm_g = 1.0 + 0.02 * jax.random.normal(ks[3], (DEPTH, HEAD_DIM), jnp.float32)
    k_norm_g = 1.0 + 0.02 * jax.random.normal(ks[4], (DEPTH, HEAD_DIM), jnp.float32)
    rel_bias = 0.1 * jax.random.normal(ks[5], (DEPTH, N_HEADS_CH, N_REL), jnp.float32)
    w_out = jax.random.normal(ks[6], (DEPTH, D_MIX, D_MODEL), jnp.float32) * D_MIX ** -0.5
    return {"x": x, "norm_g": norm_g, "w_in": w_in, "q_norm_g": q_norm_g,
            "k_norm_g": k_norm_g, "rel_bias": rel_bias, "w_out": w_out}

def first_block(x, norm_g, w_in, q_norm_g, k_norm_g, rel_bias, w_out):
    splits = np.cumsum([D_SB, D_SB, D_SB, D_SB, D_CH, D_CH, D_CH])
    for layer in range(DEPTH):
        h = rms_norm(x, norm_g[layer])
        proj = jnp.einsum('bsd,de->bse', h, w_in[layer])
        qa, ka, va, ga, qb, kb, vb, gb = jnp.split(proj, splits, axis=-1)
        ya = stick_breaking_attention(split_heads(qa, N_HEADS_SB),
                                      split_heads(ka, N_HEADS_SB),
                                      split_heads(va, N_HEADS_SB))
        yb = chunk_band_attention(split_heads(qb, N_HEADS_CH),
                                  split_heads(kb, N_HEADS_CH),
                                  split_heads(vb, N_HEADS_CH),
                                  q_norm_g[layer], k_norm_g[layer], rel_bias[layer])
        mixed = jnp.concatenate([merge_heads(ya) * jax.nn.silu(ga),
                                 merge_heads(yb) * jax.nn.silu(gb)], axis=-1)
        x = x + jnp.einsum('bse,ed->bsd', mixed, w_out[layer])
    return x


MLA_NOPE = 128
MLA_ROPE = 64
MLA_V = 128
MLA_HEADS = D_MODEL // MLA_V
MLA_Q_RANK = 768
MLA_KV_RANK = 512
MLA_QK = MLA_NOPE + MLA_ROPE
ROPE_THETA = 10000.0
SWA_HEAD_DIM = 64
SWA_HEADS = D_MODEL // SWA_HEAD_DIM
SWA_KV_HEADS = 4
SWA_GROUP = SWA_HEADS // SWA_KV_HEADS
WINDOW = 128
BLOCK = 128
REL_BUCKETS = 32
REL_MAX_DIST = 128
D_FF = 5632
CONV_WIDTH = 3
EPS = 1e-6
NEG = -1e30

MLA_IN = MLA_Q_RANK + MLA_KV_RANK + MLA_ROPE
SWA_Q = SWA_HEADS * SWA_HEAD_DIM
SWA_KV = SWA_KV_HEADS * SWA_HEAD_DIM
N_BRANCH = 2
IN_COLS = MLA_IN + SWA_Q + 2 * SWA_KV + N_BRANCH * D_MODEL


def rms_norm_2(x, g):
    xf = x.astype(jnp.float32)
    y = xf * lax.rsqrt(jnp.mean(xf * xf, axis=-1, keepdims=True) + EPS)
    return (y * g.astype(jnp.float32)).astype(x.dtype)

def rope_tables(seq):
    pos = jnp.arange(seq, dtype=jnp.float32)
    inv = ROPE_THETA ** (-jnp.arange(0, MLA_ROPE, 2, dtype=jnp.float32) / MLA_ROPE)
    ang = pos[:, None] * inv[None, :]
    ang = jnp.concatenate([ang, ang], axis=-1)
    return jnp.cos(ang), jnp.sin(ang)

def apply_rope(x, cos, sin):
    half = x.shape[-1] // 2
    x1, x2 = x[..., :half], x[..., half:]
    rot = jnp.concatenate([-x2, x1], axis=-1)
    return x * cos.astype(x.dtype) + rot * sin.astype(x.dtype)

def t5_bucket(dist):
    max_exact = REL_BUCKETS // 2
    n = jnp.maximum(dist, 0)
    large = max_exact + (jnp.log(jnp.maximum(n, 1).astype(jnp.float32) / max_exact)
                         / math.log(REL_MAX_DIST / max_exact)
                         * (REL_BUCKETS - max_exact)).astype(jnp.int32)
    large = jnp.minimum(large, REL_BUCKETS - 1)
    return jnp.where(n < max_exact, n, large)

def mla_branch(cq, ckv, k_rope, g_q, w_uq, g_kv, w_ukv):
    B, S, _ = cq.shape
    nb = S // BLOCK
    cos, sin = rope_tables(S)
    q = (rms_norm_2(cq, g_q) @ w_uq).reshape(B, S, MLA_HEADS, MLA_QK)
    q_nope = q[..., :MLA_NOPE]
    q_rope = apply_rope(q[..., MLA_NOPE:], cos[:, None, :], sin[:, None, :])
    kv = (rms_norm_2(ckv, g_kv) @ w_ukv).reshape(B, S, MLA_HEADS, MLA_NOPE + MLA_V)
    k_nope, v = kv[..., :MLA_NOPE], kv[..., MLA_NOPE:]
    k_rope = apply_rope(k_rope, cos, sin)
    scale = MLA_QK ** -0.5
    qn_blocks = q_nope.reshape(B, nb, BLOCK, MLA_HEADS, MLA_NOPE).transpose(1, 0, 2, 3, 4)
    qr_blocks = q_rope.reshape(B, nb, BLOCK, MLA_HEADS, MLA_ROPE).transpose(1, 0, 2, 3, 4)
    kpos = jnp.arange(S)

    def one_block(args):
        qn, qr, i = args
        s = (jnp.einsum('bqhd,bkhd->bhqk', qn, k_nope)
             + jnp.einsum('bqhd,bkd->bhqk', qr, k_rope)).astype(jnp.float32) * scale
        qpos = i * BLOCK + jnp.arange(BLOCK)
        s = jnp.where(kpos[None, :] <= qpos[:, None], s, NEG)
        p = jax.nn.softmax(s, axis=-1).astype(v.dtype)
        return jnp.einsum('bhqk,bkhd->bqhd', p, v)

    out = lax.map(one_block, (qn_blocks, qr_blocks, jnp.arange(nb)))
    return out.transpose(1, 0, 2, 3, 4).reshape(B, S, MLA_HEADS * MLA_V)

def swa_branch(q, k, v, rel_bias, sinks):
    B, S, _ = q.shape
    nb = S // BLOCK
    q = q.reshape(B, nb, BLOCK, SWA_KV_HEADS, SWA_GROUP, SWA_HEAD_DIM)

    def band(t):
        t = t.reshape(B, S, SWA_KV_HEADS, SWA_HEAD_DIM)
        t = jnp.pad(t, ((0, 0), (BLOCK, 0), (0, 0), (0, 0)))
        t = t.reshape(B, nb + 1, BLOCK, SWA_KV_HEADS, SWA_HEAD_DIM)
        return jnp.concatenate([t[:, :-1], t[:, 1:]], axis=2)

    kb, vb = band(k), band(v)
    s = jnp.einsum('bnqhgd,bnshd->bhgnqs', q, kb).astype(jnp.float32) * (SWA_HEAD_DIM ** -0.5)
    a = jnp.arange(BLOCK)
    bidx = jnp.arange(2 * BLOCK)
    dist = BLOCK + a[:, None] - bidx[None, :]
    bias = rel_bias[t5_bucket(dist)].astype(jnp.float32)
    bias = bias.transpose(2, 0, 1).reshape(SWA_KV_HEADS, SWA_GROUP, 1, BLOCK, 2 * BLOCK)
    kpos = jnp.arange(nb)[:, None, None] * BLOCK - BLOCK + bidx[None, None, :]
    mask = (dist >= 0)[None] & (dist < WINDOW)[None] & (kpos >= 0)
    s = jnp.where(mask, s + bias, NEG)
    sink = sinks.astype(jnp.float32).reshape(SWA_KV_HEADS, SWA_GROUP, 1, 1, 1)
    m = jnp.maximum(jnp.max(s, axis=-1, keepdims=True), sink)
    e = jnp.exp(s - m)
    p = e / (jnp.sum(e, axis=-1, keepdims=True) + jnp.exp(sink - m))
    o = jnp.einsum('bhgnqs,bnshd->bnqhgd', p.astype(vb.dtype), vb)
    return o.reshape(B, S, SWA_Q)

def causal_dwconv(u, w, b):
    S = u.shape[1]
    up = jnp.pad(u, ((0, 0), (CONV_WIDTH - 1, 0), (0, 0)))
    y = b
    for j in range(CONV_WIDTH):
        y = y + w[j] * up[:, j:j + S]
    return y

def second_inputs(seed: int = 0) -> dict:
    key = jax.random.key(seed)
    ks = jax.random.split(key, 24)
    f32 = jnp.float32
    D, L = D_MODEL, DEPTH

    def nrm(k, shape, scale):
        return jax.random.normal(k, shape, f32) * scale

    def gain(k, shape):
        return 1.0 + 0.1 * jax.random.normal(k, shape, f32)

    return {
        "x": nrm(ks[0], (BATCH, SEQ, D), 1.0),
        "c": nrm(ks[1], (BATCH, D), 1.0),
        "w_ada": nrm(ks[2], (L, D, 6 * D), 0.5 * D ** -0.5),
        "b_ada": nrm(ks[3], (L, 6 * D), 0.02),
        "g_pre_mix": gain(ks[4], (L, D)),
        "g_post_mix": gain(ks[5], (L, D)),
        "w_in": nrm(ks[6], (L, D, IN_COLS), D ** -0.5),
        "g_q_lat": gain(ks[7], (L, MLA_Q_RANK)),
        "w_uq": nrm(ks[8], (L, MLA_Q_RANK, MLA_HEADS * MLA_QK), MLA_Q_RANK ** -0.5),
        "g_kv_lat": gain(ks[9], (L, MLA_KV_RANK)),
        "w_ukv": nrm(ks[10], (L, MLA_KV_RANK, MLA_HEADS * (MLA_NOPE + MLA_V)), MLA_KV_RANK ** -0.5),
        "rel_bias": nrm(ks[11], (REL_BUCKETS, SWA_HEADS), 0.5),
        "sinks": nrm(ks[12], (L, SWA_HEADS), 1.0),
        "w_o": nrm(ks[13], (L, D, D), D ** -0.5),
        "g_pre_ffn": gain(ks[14], (L, D)),
        "g_post_ffn": gain(ks[15], (L, D)),
        "w_up": nrm(ks[16], (L, D, 2 * D_FF), D ** -0.5),
        "conv_w": nrm(ks[17], (L, CONV_WIDTH, 2 * D_FF), CONV_WIDTH ** -0.5),
        "conv_b": nrm(ks[18], (L, 2 * D_FF), 0.02),
        "w_down": nrm(ks[19], (L, D_FF, D), D_FF ** -0.5),
    }

def second_block(x, c, w_ada, b_ada, g_pre_mix, g_post_mix, w_in, g_q_lat, w_uq, g_kv_lat,
              w_ukv, rel_bias, sinks, w_o, g_pre_ffn, g_post_ffn, w_up, conv_w, conv_b, w_down):
    D = D_MODEL
    c_act = jax.nn.silu(c)
    for l in range(DEPTH):
        mod = (c_act @ w_ada[l] + b_ada[l])[:, None, :]
        sh1, sc1, gt1, sh2, sc2, gt2 = jnp.split(mod, 6, axis=-1)

        h = rms_norm_2(x, g_pre_mix[l]) * (1.0 + sc1) + sh1
        z = h @ w_in[l]
        o0 = 0
        cq = z[..., o0:o0 + MLA_Q_RANK]; o0 += MLA_Q_RANK
        ckv = z[..., o0:o0 + MLA_KV_RANK]; o0 += MLA_KV_RANK
        kr = z[..., o0:o0 + MLA_ROPE]; o0 += MLA_ROPE
        qs = z[..., o0:o0 + SWA_Q]; o0 += SWA_Q
        ks_ = z[..., o0:o0 + SWA_KV]; o0 += SWA_KV
        vs = z[..., o0:o0 + SWA_KV]; o0 += SWA_KV
        gates = jax.nn.sigmoid(z[..., o0:o0 + N_BRANCH * D])
        g_a, g_b = gates[..., :D], gates[..., D:]

        o_a = mla_branch(cq, ckv, kr, g_q_lat[l], w_uq[l], g_kv_lat[l], w_ukv[l])
        o_b = swa_branch(qs, ks_, vs, rel_bias, sinks[l])
        mix = (g_a * o_a + g_b * o_b) @ w_o[l]
        x = x + gt1 * rms_norm_2(mix, g_post_mix[l])

        h = rms_norm_2(x, g_pre_ffn[l]) * (1.0 + sc2) + sh2
        u = causal_dwconv(h @ w_up[l], conv_w[l], conv_b[l])
        y = (jax.nn.silu(u[..., :D_FF]) * u[..., D_FF:]) @ w_down[l]
        x = x + gt2 * rms_norm_2(y, g_post_ffn[l])
    return x


def setup_inputs(seed=0):
    out = dict(first_inputs(seed))
    for name, value in second_inputs(seed + 1).items():
        if name != "x":
            out[name + "_2"] = value
    return out


def reference(
    x, norm_g, w_in, q_norm_g, k_norm_g, rel_bias, w_out, c_2, w_ada_2, b_ada_2, g_pre_mix_2,
    g_post_mix_2, w_in_2, g_q_lat_2, w_uq_2, g_kv_lat_2, w_ukv_2, rel_bias_2, sinks_2, w_o_2,
    g_pre_ffn_2, g_post_ffn_2, w_up_2, conv_w_2, conv_b_2, w_down_2,
):
    x = first_block(
        x, norm_g, w_in, q_norm_g, k_norm_g, rel_bias, w_out,
    )
    return second_block(
        x, c_2, w_ada_2, b_ada_2, g_pre_mix_2, g_post_mix_2, w_in_2, g_q_lat_2, w_uq_2,
        g_kv_lat_2, w_ukv_2, rel_bias_2, sinks_2, w_o_2, g_pre_ffn_2, g_post_ffn_2, w_up_2,
        conv_w_2, conv_b_2, w_down_2,
    )


_drawn_inputs = setup_inputs


def setup_inputs(seed=0):
    import zlib

    import numpy as np

    out = dict(_drawn_inputs(seed))
    spreads = {}
    factors = {'norm_g': 6.122,
     'q_norm_g': 8.0,
     'k_norm_g': 8.0,
     'rel_bias': 8.0,
     'g_q_lat_2': 50.392,
     'g_kv_lat_2': 23.096,
     'sinks_2': 56.128,
     'conv_b_2': 200.0,
     'c_2': 3.509,
     'w_ada_2': 3.298,
     'b_ada_2': 8.0,
     'g_pre_mix_2': 8.0,
     'g_post_mix_2': 8.0,
     'w_in_2': 4.818,
     'w_uq_2': 5.144,
     'w_ukv_2': 4.839,
     'rel_bias_2': 44.38,
     'w_o_2': 4.82,
     'g_pre_ffn_2': 8.0,
     'g_post_ffn_2': 8.0,
     'w_up_2': 4.689,
     'conv_w_2': 4.679,
     'w_down_2': 4.686}
    for name, (base, spread) in spreads.items():
        noise = np.random.default_rng([zlib.crc32(name.encode()), seed]).standard_normal(out[name].shape)
        drawn = base * np.exp(spread * noise) if base else spread * noise
        out[name] = __import__('jax').numpy.asarray(drawn.astype(out[name].dtype))
    for name, factor in factors.items():
        out[name] = (out[name] * factor).astype(out[name].dtype)
    return out
```

```python
from contextlib import ExitStack, contextmanager

import numpy as np

import concourse.bass as bass
from concourse import mybir

F32 = mybir.dt.float32
F32R = mybir.dt.float32r
BF16 = mybir.dt.bfloat16
ALU = mybir.AluOpType
ACT = mybir.ActivationFunctionType
AX = mybir.AxisListType
ds = bass.ds

P = 128
SEQ = 256
ST = SEQ // P
D = 2048
KT = D // P
PANEL = 512
SLOTS = KT // 2
AHEAD = 3
RING = 4
EPS = 1e-6
NEG = -1e30

HD = 128
N_A = N_B = 8
CHUNK = 64
REL_CLIP = 256
N_REL = REL_CLIP + CHUNK
MLA_H, ROPE, Q_RANK, KV_RANK = 16, 64, 768, 512
QT, VT = Q_RANK // P, KV_RANK // P
LAT = Q_RANK + KV_RANK + ROPE
SWA_H, SWA_G, SWA_D, WINDOW, BUCKETS = 32, 4, 64, 128, 32
BAND = 2 * WINDOW
FF = 5632
FT = FF // P
TOEP = 384

C_NORM, C_PREMIX, C_POSTMIX, C_PREFFN, C_POSTFFN, C_C, C_QLAT, C_KVLAT, C_QN, C_KN = (
    0, 16, 32, 48, 64, 80, 96, 102, 106, 107)
C_ADA, C_CONVB, C_CONVW = 128, 256, 384
PARAM_ROWS = [108, 96, FT * 2, FT * 2, FT * 2, FT * 2]

SH1, SC1, GT1, SH2, SC2, GT2 = range(6)


class Tally:

    def __init__(self, eng, credits):
        self.eng, self.credits = eng, credits
        self.count, self.stride, self.i = {}, None, None

    def _next(self, key, k):
        self.count[key] = self.count.get(key, 0) + k
        n = self.count[key]
        if self.i is not None and key in self.stride:
            n = self.i * self.stride[key] + n
        elif self.i is not None and k:
            raise ValueError(f"no stride for {key}")
        return n

    def ready(self, sem, k=1):
        return self._next(("ready", sem.name), k) + self.credits.get(sem.name, 0)

    def free(self, sem, k=1):
        return self._next(("free", sem.name), k)

    def skip(self, sem, k=1, what="ready"):
        self._next((what, sem.name), k)

    @contextmanager
    def loop(self, n, **strides):
        keys = {}
        for name, k in strides.items():
            what, sem = name.split("_", 1)
            keys[(what, sem)] = k
        before = dict(self.count)
        with self.eng.Fori(0, n) as i:
            self.i, self.stride = i, keys
            yield i
            self.i = None
        for key in {*self.count, *keys}:
            moved = self.count.get(key, 0) - before.get(key, 0)
            if moved != keys.get(key, 0):
                raise ValueError(f"{key}: moved {moved}, stride {keys.get(key, 0)}")
            self.count[key] = before.get(key, 0) + n * moved


def block_kernel(nc, x, norm_g, w_in, q_norm_g, k_norm_g, rel_bias, w_out, c_2, w_ada_2, b_ada_2,
                 g_pre_mix_2, g_post_mix_2, w_in_2, g_q_lat_2, w_uq_2, g_kv_lat_2, w_ukv_2,
                 rel_bias_2, sinks_2, w_o_2, g_pre_ffn_2, g_post_ffn_2, w_up_2, conv_w_2, conv_b_2,
                 w_down_2, rope_cos, rope_sin, bucket_hot, out):
    ctx = ExitStack()
    with ctx:
        def sb(name, shape, dt=F32):
            return ctx.enter_context(nc.sbuf_tensor(name, shape, dt))

        semaphores = {}
        credits = {"chunk_used": RING, "acc_free0": 1, "acc_free1": 1,
                   "ada_done": 2, "qk_transposed": 1, "qkT_full": 1, "scores_done": 1, "s_read": 1,
                   "p_transposed": 1, "pT_full": 1, "o_ready": 1, "o_done": 1,
                   "bias_used": 2, "up_free": 4,
                   "sb_w_done": 2, "sb_o_ready": 1, "sb_o_done": 1, "sb_transposed": 1, "sb_qkT": 1,
                   "sb_zdone": 1, "sb_cum": 1}

        def sem(name):
            s = ctx.enter_context(nc.semaphore(name))
            semaphores[name] = s
            return s

        raw = sb("raw", [P, 2, 2048])
        w_hi = sb("w_hi", [P, RING, 1024], F32R)
        w_lo = sb("w_lo", [P, RING, 1024], F32R)
        aT_hi = sb("aT_hi", [P, KT, SEQ], F32R)
        aT_lo = sb("aT_lo", [P, KT, SEQ], F32R)
        latT_hi = sb("latT_hi", [P, QT + VT, SEQ], F32R)
        latT_lo = sb("latT_lo", [P, QT + VT, SEQ], F32R)
        ada_raw = sb("ada_raw", [P, 2, 1024])
        arena = sb("arena", [P, 19584])

        def rows(at, width):
            return arena[:, at:at + ST * width].rearrange("p (s n) -> p s n", s=ST)

        X = rows(0, D)
        H = rows(4096, D)
        QKV_B = rows(0, 3 * N_B * HD)
        QKV_A = rows(6144, 3 * N_A * HD)
        ADA_ACC = [arena[:, 12288 + 2048 * j:12288 + 2048 * (j + 1)] for j in range(3)]
        PARAM = arena[:, 16384:16384 + 768].rearrange("p (t n) -> p t n", t=6)
        Q = rows(0, MLA_H * (HD + ROPE))
        KV = rows(6144, MLA_H * 2 * HD)
        LATR = rows(6144, LAT)
        LATN = rows(10240, LAT)
        QS = rows(14336, SWA_H * SWA_D)
        KVS = rows(18432, 2 * SWA_G * SWA_D)
        KR = rows(19456, ROPE)
        MIX = rows(4096, D)
        G_MIX = arena[:, 8192:8192 + D]
        G_FFN = arena[:, 4096:4096 + D]
        H_FFN = rows(6144, D)
        YT = arena[:, 6144:6144 + FT * SEQ].rearrange("p (f t) -> p f t", f=FT)
        ADA_FFN = arena[:, 17408:17408 + 2048]
        ADA_MIX = arena[:, 12288:12288 + 2048]

        stage = sb("stage", [P, ST, 2, HD])
        ROPE_BUF = ada_raw[:, :, :].rearrange("p a n -> p (a n)")
        stage_r, tmp_r, cosT, sinT = [ROPE_BUF[:, P * j:P * (j + 1)].rearrange("p (s n) -> p s n", s=ST)
                                      for j in range(4)]
        qrT, krT = ROPE_BUF[0:ROPE, 512:512 + SEQ], ROPE_BUF[0:ROPE, 768:768 + SEQ]
        qkT = sb("qkT", [P, 2 * SEQ])
        s_sb = sb("s_sb", [P, 2, 384])
        pT = sb("pT", [P, 2, 384])
        bias = sb("bias", [P, 1024])
        ident = sb("ident", [P, P])
        ident_b = sb("ident_b", [P, P], BF16)
        tri = sb("tri", [P, P])
        minus1 = sb("minus1", [P, P])
        below = sb("below", [P, P])
        neg_b = sb("neg_b", [P, P], BF16)
        ones = sb("ones", [P, P])
        col = sb("col", [P, 6 * P])
        mod = sb("mod", [P, 6, KT])
        silu_c = sb("silu_c", [P, KT])
        gains = sb("gains", [P, 4, KT])
        zero_c = sb("zero_c", [P, 1])
        stat = sb("stat", [P, 16])
        smx = sb("smx", [P, 28])
        sink = sb("sink", [P, SWA_H])
        PS = ctx.enter_context(nc.psum_tensor("PS", [P, 8, 512], F32))
        B_T, B_S1, B_S0, B_P, B_O = 2, 3, 4, 5, 7
        B_Z = ((4, 3), (6, 5))

        table = s_sb[0:BUCKETS + 1, 0, 0:SWA_H]
        hot = pT[0:BUCKETS + 1, 0, 0:383]
        expanded = pT[0:SWA_H, 1, 0:383]
        conv_g = [s_sb[:, 0, 0:SEQ], pT[:, 0, 0:SEQ]]
        conv_u = [s_sb[:, 1, 0:SEQ], pT[:, 1, 0:SEQ]]
        diag = bias[:, :].rearrange("p (b n) -> p b n", b=2)

        x1_dram = nc.dram_tensor("x1_rows", (SEQ, D), F32, kind="Internal").ap()
        win_dram = nc.dram_tensor("window_bias", (SWA_H, TOEP), F32, kind="Internal").ap()

        landed = [sem(f"landed{i}") for i in range(2)]
        hi_ready, lo_ready = sem("hi_ready"), sem("lo_ready")
        chunk_used = sem("chunk_used")
        acc_ready = sem("acc_ready")
        acc_free = [sem("acc_free0"), sem("acc_free1")]
        gate_ready = sem("gate_ready")
        ada_landed = [sem("ada_landed0"), sem("ada_landed1")]
        ada_done = sem("ada_done")
        x_landed, par_landed, misc_landed = sem("x_landed"), sem("par_landed"), sem("misc_landed")
        rope_landed = sem("rope_landed")
        bias_landed = [sem("bias_landed0"), sem("bias_landed1")]
        bias_used = sem("bias_used")
        stored = sem("stored")
        const_ready = sem("const_ready")
        mask_ready = sem("mask_ready")
        par_T, par_ready = sem("par_T"), sem("par_ready")
        silu_ready = sem("silu_ready")
        act_step, dve_step, pool_step = sem("act_step"), sem("dve_step"), sem("pool_step")
        sq_ready, var_ready, std_ready = sem("sq_ready"), sem("var_ready"), sem("std_ready")
        rows_ready = sem("rows_ready")
        rows_T = sem("rows_T")
        aT_hi_ready, aT_ready = sem("aT_hi_ready"), sem("aT_ready")
        stage_full, qk_transposed, qkT_full = sem("stage_full"), sem("qk_transposed"), sem("qkT_full")
        scores_done, s_read, nm_full = sem("scores_done"), sem("s_read"), sem("nm_full")
        p_done, p_transposed, pT_full = sem("p_done"), sem("p_transposed"), sem("pT_full")
        o_ready, o_done = sem("o_ready"), sem("o_done")
        ss_full, rs_full = sem("ss_full"), sem("rs_full")
        sb_staged, sb_transposed, sb_qkT = sem("sb_staged"), sem("sb_transposed"), sem("sb_qkT")
        sb_zdone, sb_ln, sb_spdone, sb_cum = sem("sb_zdone"), sem("sb_ln"), sem("sb_spdone"), sem("sb_cum")
        sb_w_done, sb_o_ready, sb_o_done = sem("sb_w_done"), sem("sb_o_ready"), sem("sb_o_done")
        ada_cols, mod_ready = sem("ada_cols"), sem("mod_ready")
        win_cols, win_ready, win_stored = sem("win_cols"), sem("win_ready"), sem("win_stored")
        x_saved = sem("x_saved")
        kr_staged, kr_T, kr_ready = sem("kr_staged"), sem("kr_T"), sem("kr_ready")
        diag_ready, diag_used, g_ready = sem("diag_ready"), sem("diag_used"), sem("g_ready")
        up_ready, conv_a, conv_d, conv_s, up_free = (
            sem("up_ready"), sem("conv_a"), sem("conv_d"), sem("conv_s"), sem("up_free"))
        y_hi, y_ready = sem("y_hi"), sem("y_ready")
        down_done, fin_ready = sem("down_done"), sem("fin_ready")

        def give(eng, *names):
            for name in names:
                eng.nop().then_inc(semaphores[name], credits[name])

        block = ctx.enter_context(nc.Block())
        PE_PANEL = dict(ready_lo_ready=8, free_acc_free0=1, free_acc_free1=1)
        ACT_PANEL = dict(ready_landed0=64, ready_landed1=64, free_chunk_used=8)
        DVE_PANEL = dict(ready_hi_ready=8)
        START = (0, 1, 3, 4)
        START_B = (1, 4)
        N_PANELS = 16 + 4 + 3 + 1 + 6 + 8 + 4 + 4 + 4 + 4

        @block.sync
        def _(sp):
            T = Tally(sp, credits)
            n_raw, n_ada, n_bias = [0], [0], [0]

            def load(pieces, first=False):
                m = n_raw[0]
                n_raw[0] += 1
                if not first:
                    sp.wait_ge(lo_ready, T.ready(lo_ready, 2))
                for j, src in enumerate(pieces):
                    dst = raw[:, m % 2, 1024 * j:1024 * (j + 1)]
                    if len(src.shape) == 3:
                        dst = dst.rearrange("p (k n) -> p k n", k=src.shape[1])
                    sp.dma_start(dst, src).then_inc(landed[m % 2], 16)

            def tiles(w, k0, c0, kts=2, width=PANEL):
                return w[k0:k0 + kts * P, ds(c0, width)].rearrange("(k p) n -> p k n", p=P)

            def load_panel(w, r, c0, first=False):
                load([tiles(w, 512 * r, c0), tiles(w, 512 * r + 256, c0)], first)

            def load_ada(row, c0):
                j = n_ada[0] % 2
                n_ada[0] += 1
                sp.wait_ge(ada_done, T.free(ada_done))
                sp.dma_start(ada_raw[:, j, :], w_ada_2[0, ds(row, P), c0:c0 + 1024]).then_inc(ada_landed[j], 16)

            def panel(w, c0, following, beside=None):
                for slot in range(SLOTS):
                    if slot in (0, 2):
                        load_panel(w, 2 + slot // 2, c0)
                    if slot in (4, 6):
                        following(slot // 2 - 2)
                    if beside is not None:
                        beside(slot)

            def panels(n, w, c0, following, beside=None, **strides):
                strides = dict(ready_lo_ready=8, **strides)
                if n > 1:
                    with T.loop(n - 1, **strides) as i:
                        panel(w, i * PANEL + c0, lambda r: load_panel(w, r, i * PANEL + (c0 + PANEL)),
                              None if beside is None else lambda slot: beside(i, slot))
                last = c0 + PANEL * (n - 1)
                panel(w, last, following, None if beside is None else lambda slot: beside(n - 1, slot))

            def upto(w, c0):
                return lambda r: load_panel(w, r, c0)

            W_IN, W_OUT, W_IN2, W_O = w_in[0], w_out[0], w_in_2[0], w_o_2[0]
            for s in range(ST):
                sp.dma_start(X[:, s, :], x[0, s * P:(s + 1) * P, :]).then_inc(x_landed, 16)
            for t, r, src, n in [(0, C_NORM, norm_g, KT), (0, C_PREMIX, g_pre_mix_2, KT),
                                 (0, C_POSTMIX, g_post_mix_2, KT), (0, C_PREFFN, g_pre_ffn_2, KT),
                                 (0, C_POSTFFN, g_post_ffn_2, KT), (0, C_C, c_2, KT), (0, C_QLAT, g_q_lat_2, QT),
                                 (0, C_KVLAT, g_kv_lat_2, VT), (0, C_QN, q_norm_g, 1), (0, C_KN, k_norm_g, 1),
                                 (1, 0, b_ada_2, 6 * KT), (2, 0, conv_b_2, 2 * FT),
                                 (3, 0, conv_w_2[0, 0:1, :], 2 * FT), (4, 0, conv_w_2[0, 1:2, :], 2 * FT),
                                 (5, 0, conv_w_2[0, 2:3, :], 2 * FT)]:
                sp.dma_start(PARAM[r:r + n, t, :], src.rearrange("a (r n) -> (a r) n", n=P)).then_inc(par_landed, 16)
            C_B0 = 4 * N_A * HD
            load_panel(W_IN, 0, C_B0, first=True)
            load_panel(W_IN, 1, C_B0, first=True)
            sp.dma_start(sink[:], bass.AP(sinks_2.tensor, 0, [[0, P], [1, SWA_H]])).then_inc(misc_landed, 16)
            sp.dma_start(hot, bucket_hot).then_inc(misc_landed, 16)
            sp.wait_ge(const_ready, 1)
            sp.dma_start(table[0:BUCKETS, :], rel_bias_2).then_inc(misc_landed, 16)

            def g1_ada(kt0):
                def beside(i, slot):
                    if slot < 6:
                        part = (SH1, SC1, SH2)[slot // 2]
                        load_ada(i * P + kt0 * P, part * D + 1024 * (slot % 2))
                return beside

            def chunk_bias(h):
                b = n_bias[0] % 2
                n_bias[0] += 1
                sp.wait_ge(bias_used, T.free(bias_used))
                for t in range(ST):
                    at, end = 384 * b + P * t, 384 * b + P * t + P * (t + 1)
                    for q0 in (0, CHUNK):
                        first = at + CHUNK - q0
                        src = bass.AP(rel_bias.tensor, h * N_REL, [[1, CHUNK], [1, end - first]])
                        sp.dma_start(bias[q0:q0 + CHUNK, first:end], src).then_inc(bias_landed[b], 16)

            def ada_and_bias(i, slot):
                if slot < 2:
                    chunk_bias(i * 2 + slot)
                g1_ada(6)(i, slot)

            panels(6, W_IN, C_B0, upto(W_IN, 0), g1_ada(0), free_ada_done=6)
            panels(4, W_IN, 0, upto(W_IN, 2048), ada_and_bias, free_ada_done=6, free_bias_used=2)
            panels(2, W_IN, 2048, upto(W_IN, 7168), g1_ada(10), free_ada_done=6)
            panels(2, W_IN, 7168, upto(W_IN, 3072), g1_ada(12), free_ada_done=6)
            panels(2, W_IN, 3072, upto(W_OUT, 0), g1_ada(14), free_ada_done=6)
            sp.wait_ge(rows_T, T.ready(rows_T, 16))
            for s in range(ST):
                sp.dma_start(X[:, s, :], x[0, s * P:(s + 1) * P, :]).then_inc(x_landed, 16)

            def out_ada(part):
                return lambda i, slot: load_ada(i * (4 * P) + (slot // 2) * P, part * D + 1024 * (slot % 2))

            panels(4, W_OUT, 0, upto(W_IN2, 0), out_ada(SC2), free_ada_done=8)
            sp.wait_ge(rows_ready, T.ready(rows_ready, 6))
            for s in range(ST):
                sp.dma_start(x1_dram[s * P:(s + 1) * P, :], X[:, s, :]).then_inc(x_saved, 16)
            sp.dma_start(cosT, rope_cos.rearrange("(s p) n -> p s n", p=P)).then_inc(rope_landed, 16)
            sp.dma_start(sinT, rope_sin.rearrange("(s p) n -> p s n", p=P)).then_inc(rope_landed, 16)
            C_KVS = LAT + SWA_H * SWA_D
            panels(3, W_IN2, 0, upto(W_IN2, C_KVS))
            uq = [lambda c0=c0, k=k: load([w_uq_2[0, (k + j) * P:(k + j + 1) * P, c0:c0 + 1024] for j in range(2)])
                  for c0 in range(0, MLA_H * (HD + ROPE), 1024) for k in range(0, QT, 2)]
            panels(1, W_IN2, C_KVS, lambda r: uq[r]())
            for f in uq[2:]:
                f()
            with T.loop(4, ready_lo_ready=4) as i:
                for j in range(2):
                    c0 = i * 1024 + PANEL * j
                    load([tiles(w_ukv_2[0], 0, c0), tiles(w_ukv_2[0], 2 * P, c0)])
            for r in range(2):
                load_panel(W_IN2, r, LAT)
            C_G = C_KVS + 2 * SWA_G * SWA_D
            panels(4, W_IN2, LAT, upto(W_IN2, C_G))

            def window_bias(i, slot):
                if slot >= 4:
                    return
                b = n_bias[0] % 2
                n_bias[0] += 1
                sp.wait_ge(bias_used, T.free(bias_used))
                for e in range(2):
                    src = bass.AP(win_dram.tensor, i * (8 * TOEP) + (2 * slot + e) * TOEP, [[1, P], [1, BAND]])
                    sp.dma_start(bias[:, 512 * b + BAND * e:512 * b + BAND * (e + 1)], src)\
                      .then_inc(bias_landed[b], 16)

            sp.wait_ge(win_stored, 16)
            sp.wait_ge(s_read, T.ready(s_read, N_B + MLA_H))
            panels(4, W_IN2, C_G, upto(W_IN2, C_G + D), window_bias, free_bias_used=4)
            panels(4, W_IN2, C_G + D, upto(W_O, 0))
            sp.wait_ge(x_saved, 32)
            sp.wait_ge(rows_T, T.ready(rows_T, 8 + 5 + 8))
            for s in range(ST):
                sp.dma_start(X[:, s, :], x1_dram[s * P:(s + 1) * P, :]).then_inc(x_landed, 16)

            def up_raw(r, c0):
                m = n_raw[0]
                n_raw[0] += 1
                sp.wait_ge(lo_ready, T.ready(lo_ready, 2))
                dst = raw[:, m % 2, :].rearrange("p (k h n) -> p k h n", k=4, h=2)
                for h in range(2):
                    sp.dma_start(dst[:, :, h, :], tiles(w_up_2[0], 512 * r, c0 + h * FF, 4, 256))\
                      .then_inc(landed[m % 2], 16)

            def down_raw(kt):
                load([w_down_2[0, ds(kt * P, P), 1024 * h:1024 * (h + 1)] for h in range(2)])

            panels(4, W_O, 0, lambda r: up_raw(r, 0), out_ada(GT1), free_ada_done=8)

            def up_pair(p, kt=None, last=False):
                for j in range(2):
                    for r in range(4):
                        if r < 2:
                            up_raw(2 + r, p * 256 + 256 * j)
                        elif last and j:
                            down_raw(r - 2)
                        else:
                            up_raw(r - 2, p * 256 + 256 * (j + 1))
                        if kt is not None and r < 2:
                            load_ada(kt * P + P * j, GT2 * D + 1024 * r)

            with T.loop(8, ready_lo_ready=16, free_ada_done=4) as i:
                up_pair(i * 2, i * 2)
            with T.loop(2, ready_lo_ready=16) as i:
                up_pair(i * 2 + 16)
            up_pair(20, last=True)
            with T.loop(FT // 2 - 1, ready_lo_ready=4) as i:
                for j in range(2):
                    down_raw(i * 2 + (2 + j))
            for s in range(ST):
                sp.wait_ge(fin_ready, s + 1)
                sp.dma_start(out[0, s * P:(s + 1) * P, :], X[:, s, :]).then_inc(stored, 16)
            sp.wait_ge(stored, 16 * ST)

        @block.gpsimd
        def _(pool):
            T = Tally(pool, credits)

            def select(dst, keep_if, base, channel, step, fill):
                return nc.gpsimd.affine_select(out=dst, in_=dst, compare_op=keep_if, fill=fill, base=base,
                                               pattern=[[step, dst.shape[1]]], channel_multiplier=channel)

            for k, (dst, v) in enumerate(((ident, 0.0), (ident_b, 0.0), (tri, -1.0), (below, 1.0), (neg_b, NEG),
                                          (ones, 1.0), (minus1, -1.0), (zero_c, 0.0))):
                nc.gpsimd.memset(dst[:], v).then_inc(pool_step, 1)
            nc.gpsimd.memset(bias[:], NEG).then_inc(pool_step, 1)
            nc.gpsimd.memset(table, NEG).then_inc(pool_step, 1)
            pool.wait_ge(pool_step, 10)
            select(ident[:], ALU.not_equal, 0, 1, -1, 1.0).then_inc(pool_step, 1)
            select(ident_b[:], ALU.not_equal, 0, 1, -1, 1.0).then_inc(pool_step, 1)
            select(tri[:], ALU.is_ge, 0, 1, -1, 0.0).then_inc(pool_step, 1)
            select(below[:], ALU.is_gt, 0, -1, 1, 0.0).then_inc(pool_step, 1)
            select(neg_b[:], ALU.is_ge, 0, 1, -1, 0.0).then_inc(pool_step, 1)
            pool.wait_ge(pool_step, 15)
            nc.gpsimd.nop().then_inc(const_ready, 1)
            pool.wait_ge(win_ready, 1)
            nc.gpsimd.dma_start(win_dram[:, 0:383], expanded).then_inc(win_stored, 16)

            def stage_sb(h):
                pool.wait_ge(sb_transposed, T.free(sb_transposed))
                nc.gpsimd.tensor_copy(stage[:, :, 0, :], QKV_A[:, :, ds(h * HD, HD)])
                nc.gpsimd.tensor_copy(stage[:, :, 1, :], QKV_A[:, :, ds(h * HD + N_A * HD, HD)])\
                    .then_inc(sb_staged, 1)

            pool.wait_ge(acc_free[1], credits["acc_free1"] + 12)
            pool.wait_ge(qk_transposed, credits["qk_transposed"] + N_B)
            with T.loop(2, free_sb_transposed=4) as i:
                for j in range(4):
                    stage_sb(i * 4 + j)

            pool.wait_ge(s_read, credits["s_read"] + N_B)
            nc.gpsimd.memset(bias[:, 0:384], 0.0).then_inc(pool_step, 1)
            pool.wait_ge(pool_step, 16)
            select(bias[:, 0:P], ALU.is_ge, 0, 1, -1, NEG).then_inc(mask_ready, 1)
            select(bias[:, 2 * P:3 * P], ALU.is_ge, 0, 1, -1, NEG).then_inc(mask_ready, 1)

            def rope(dst, src, done):
                half = ROPE // 2
                nc.gpsimd.tensor_tensor(tmp_r[:, :, 0:half], src[:, :, half:ROPE], sinT[:, :, 0:half], ALU.mult)
                nc.gpsimd.tensor_tensor(tmp_r[:, :, half:ROPE], src[:, :, 0:half], sinT[:, :, half:ROPE], ALU.mult)
                nc.gpsimd.tensor_tensor(dst, src, cosT, ALU.mult).then_inc(pool_step, 1)
                pool.wait_ge(pool_step, T.ready(pool_step))
                nc.gpsimd.tensor_tensor(dst, dst, tmp_r, ALU.add).then_inc(done, 1)

            T.skip(pool_step, 16)
            pool.wait_ge(rope_landed, 32)
            pool.wait_ge(acc_free[1], credits["acc_free1"] + 16 + 4 + 3)
            rope(stage_r, KR[:], kr_staged)
            pool.wait_ge(kr_T, 1)

            def stage_mla(h):
                pool.wait_ge(qk_transposed, T.free(qk_transposed))
                nc.gpsimd.tensor_copy(stage[:, :, 0, :], Q[:, :, ds(h * (HD + ROPE), HD)])
                nc.gpsimd.tensor_copy(stage[:, :, 1, :], KV[:, :, ds(h * (2 * HD), HD)])
                rope(stage_r, Q[:, :, ds(h * (HD + ROPE) + HD, ROPE)], stage_full)

            pool.wait_ge(acc_free[1], credits["acc_free1"] + 16 + 4 + 4 + 6 + 8)
            T.skip(qk_transposed, N_B, "free")
            with T.loop(4, free_qk_transposed=4, ready_pool_step=4) as i:
                for j in range(4):
                    stage_mla(i * 4 + j)

            def stage_swa(pair, group):
                pool.wait_ge(qk_transposed, T.free(qk_transposed))
                nc.gpsimd.tensor_copy(stage[:, :, 0, :], QS[:, :, ds(pair * P, P)])
                for e in range(2):
                    last = nc.gpsimd.tensor_copy(stage[:, :, 1, e * SWA_D:(e + 1) * SWA_D],
                                                 KVS[:, :, ds(group * SWA_D, SWA_D)])
                last.then_inc(stage_full, 1)

            pool.wait_ge(acc_free[1], credits["acc_free1"] + 16 + 4 + 4 + 6 + 8 + 4)
            with T.loop(4, free_qk_transposed=4) as i:
                for j in range(4):
                    stage_swa(i * 4 + j, i)

        @block.scalar
        def _(act):
            T = Tally(act, credits)
            n = [0]

            def split():
                m = n[0]
                n[0] += 1
                if m % 2 == 0:
                    act.wait_ge(landed[m // 2 % 2], T.ready(landed[m // 2 % 2], 32))
                act.wait_ge(chunk_used, T.free(chunk_used))
                nc.scalar.activation(w_hi[:, m % RING, :], raw[:, m // 2 % 2, 1024 * (m % 2):1024 * (m % 2 + 1)],
                                     ACT.Copy).then_inc(hi_ready, 1)

            give(act, "qkT_full", "pT_full", "sb_qkT", "sb_w_done")
            nc.scalar.preload_act_table_set("natural_log_exp_and_others")

            def rms(src, width, at):
                act.wait_ge(sq_ready, T.ready(sq_ready))
                for s in range(ST):
                    nc.scalar.activation(PS[:, B_T:B_T + 4, :].rearrange("p b n -> p (b n)")[:, 0:width],
                                         src[:, s, 0:width], ACT.Square,
                                         accum_out=stat[:, at + s:at + s + 1]).then_inc(act_step, 1)
                    act.wait_ge(act_step, T.ready(act_step))
                nc.scalar.nop().then_inc(var_ready, 1)

            def root(at):
                act.wait_ge(std_ready, T.ready(std_ready))
                nc.scalar.activation(stat[:, at:at + ST], stat[:, at:at + ST], ACT.Sqrt).then_inc(var_ready, 1)

            def columns_hi(groups, dst, kts, gain=None, shift=None):
                for j in range(groups):
                    act.wait_ge(rows_T, T.ready(rows_T))
                    bank = PS[:, B_T + j % 4, :]
                    if gain is None:
                        last = nc.scalar.activation(dst[:, 2 * j:2 * j + 2, :].rearrange("p k t -> p (k t)"), bank,
                                                    ACT.Copy)
                    else:
                        for k in range(2):
                            last = nc.scalar.activation(dst[:, 2 * j + k, :], bank[:, SEQ * k:SEQ * (k + 1)],
                                                        ACT.Identity, bias=shift(2 * j + k), scale=gain(2 * j + k))
                    last.then_inc(aT_hi_ready, 1)

            def after_T(kind):
                act.wait_ge(qk_transposed, T.ready(qk_transposed))
                act.wait_ge(scores_done, T.free(scores_done))
                if kind == "b":
                    nc.scalar.activation(qkT[:, 0:SEQ], PS[:, B_T, 0:SEQ], ACT.Copy, scale=col[:, C_QN:C_QN + 1])
                    last = nc.scalar.activation(qkT[:, SEQ:], PS[:, B_T, SEQ:], ACT.Copy, scale=col[:, C_KN:C_KN + 1])
                else:
                    if kind == "mla":
                        nc.scalar.activation(qrT, PS[0:ROPE, B_S1, 0:SEQ], ACT.Copy)
                    last = nc.scalar.activation(qkT[:], PS[:, B_T, :], ACT.Copy)
                last.then_inc(qkT_full, 1)

            def after_S(kind, pair=None):
                act.wait_ge(nm_full, T.ready(nm_full))
                act.wait_ge(p_transposed, T.free(p_transposed))
                for e in range(2 if kind == "swa" else 1):
                    if kind == "swa":
                        nc.scalar.activation(smx[:, 12 + 2 * e:14 + 2 * e], smx[:, 4 + 2 * e:6 + 2 * e], ACT.Exp,
                                             bias=sink[:, ds(pair * 2 + e, 1)])
                    for t, (a, b) in enumerate(((0, P), (P, 384))):
                        last = nc.scalar.activation(s_sb[:, e, a:b], s_sb[:, e, a:b], ACT.Exp,
                                                    bias=smx[:, 4 + 2 * e + t:5 + 2 * e + t],
                                                    accum_out=smx[:, 8 + 2 * e + t:9 + 2 * e + t])
                last.then_inc(p_done, 1)

            def after_P(kind):
                act.wait_ge(p_transposed, T.ready(p_transposed))
                act.wait_ge(o_ready, T.free(o_ready))
                for e in range(2 if kind == "swa" else 1):
                    last = nc.scalar.activation(pT[:, e, :], PS[:, B_P + e, 0:384], ACT.Copy)
                last.then_inc(pT_full, 1)

            def rms_b():
                act.wait_ge(ss_full, T.ready(ss_full))
                nc.scalar.activation(stat[:, 8:12], stat[:, 8:12], ACT.Ln).then_inc(act_step, 1)
                act.wait_ge(act_step, T.ready(act_step))
                nc.scalar.activation(stat[:, 8:12], stat[:, 8:12], ACT.Exp, scale=-0.5).then_inc(rs_full, 1)

            def sb_T():
                act.wait_ge(sb_transposed, T.ready(sb_transposed))
                act.wait_ge(sb_zdone, T.free(sb_zdone))
                nc.scalar.activation(qkT[:, 0:SEQ], PS[:, B_T, 0:SEQ], ACT.Copy, scale=float(HD ** -0.5))
                nc.scalar.activation(qkT[:, SEQ:], PS[:, B_T, SEQ:], ACT.Copy).then_inc(sb_qkT, 1)

            def sb_Z(b):
                act.wait_ge(sb_zdone, T.ready(sb_zdone))
                act.wait_ge(sb_cum, T.free(sb_cum))
                for e, w in ((0, SEQ), (1, P)):
                    nc.scalar.activation(s_sb[:, e, 0:w], PS[:, B_Z[b][e], 0:w], ACT.Abs).then_inc(act_step, 1)
                act.wait_ge(act_step, T.ready(act_step, 2))
                for e, w in ((0, SEQ), (1, P)):
                    nc.scalar.activation(s_sb[:, e, 0:w], s_sb[:, e, 0:w], ACT.Exp, scale=-1.0).then_inc(act_step, 1)
                act.wait_ge(act_step, T.ready(act_step, 2))
                for e, w in ((0, SEQ), (1, P)):
                    last = nc.scalar.activation(s_sb[:, e, 0:w], s_sb[:, e, 0:w], ACT.Ln, bias=1.0)
                last.then_inc(sb_ln, 1)

            def sb_C(b):
                act.wait_ge(sb_cum, T.ready(sb_cum))
                act.wait_ge(sb_o_ready, T.free(sb_o_ready))
                nc.scalar.activation(pT[:, 0, 0:SEQ], PS[:, B_Z[b][0], 0:SEQ], ACT.Exp)
                nc.scalar.activation(pT[:, 1, 0:P], PS[:, B_Z[b][1], 0:P], ACT.Exp).then_inc(sb_w_done, 1)

            def products(s, chunks=SLOTS):
                if s == 0:
                    act.wait_ge(acc_ready, T.ready(acc_ready))
                else:
                    act.wait_ge(chunk_used, T.ready(chunk_used, chunks))

            def gate(func):
                for s in range(ST):
                    products(s)
                    nc.scalar.activation(PS[:, s, :], PS[:, s, :], func).then_inc(gate_ready, 1)

            SP_ = ACT_PANEL
            act.wait_ge(x_landed, 32)
            rms(X, D, 0)
            root(0)
            for _ in range(AHEAD):
                split()
            act.wait_ge(par_ready, 1)
            act.wait_ge(const_ready, 1)
            nc.scalar.activation(silu_c[:], col[:, C_C:C_C + KT], ACT.Silu).then_inc(silu_ready, 1)
            columns_hi(8, aT_hi, KT, gain=lambda k: col[:, C_NORM + k:C_NORM + k + 1], shift=lambda k: zero_c[:])
            with T.loop(6, **SP_) as i:
                for slot in range(SLOTS):
                    split()
            T.skip(acc_ready, 12)
            T.skip(chunk_used, 12 * SLOTS)
            act.wait_ge(win_stored, 16)
            nc.scalar.preload_act_table_set("natural_log_exp_and_others")
            with T.loop(4, **SP_, ready_ss_full=2, ready_act_step=2, ready_qk_transposed=2, free_scores_done=2,
                        ready_nm_full=2, ready_p_transposed=2, free_p_transposed=2, free_o_ready=2) as i:
                for slot in range(SLOTS):
                    split()
                    if slot - 2 in START_B:
                        after_P("b")
                    if slot - 1 in START_B:
                        after_S("b")
                    if slot in START_B:
                        after_T("b")
                    if slot + 1 in START_B:
                        rms_b()
            with T.loop(2, **SP_) as i:
                for slot in range(SLOTS):
                    split()
            GATED = dict(**SP_, ready_acc_ready=1, ready_chunk_used=8)
            with T.loop(2, **GATED, ready_act_step=16, ready_sb_transposed=4, free_sb_zdone=4, ready_sb_zdone=4,
                        free_sb_cum=4, ready_sb_cum=4, free_sb_o_ready=4) as i:
                for slot in range(SLOTS):
                    split()
                    if slot - 2 in START:
                        sb_C(START.index(slot - 2) % 2)
                    if slot - 1 in START:
                        sb_Z(START.index(slot - 1) % 2)
                    if slot in START:
                        sb_T()
                gate(ACT.Silu)
            with T.loop(2, **GATED) as i:
                for slot in range(SLOTS):
                    split()
                gate(ACT.Silu)
            columns_hi(8, aT_hi, KT)
            with T.loop(4, **SP_) as i:
                for slot in range(SLOTS):
                    split()
            rms(X, D, 0)
            root(0)
            act.wait_ge(mod_ready, T.ready(mod_ready, 5))
            columns_hi(8, aT_hi, KT, gain=lambda k: gains[:, 0, k:k + 1], shift=lambda k: mod[:, SH1, k:k + 1])
            with T.loop(3, **SP_) as i:
                for slot in range(SLOTS):
                    split()
            rms(LATR, Q_RANK, 2)
            rms(LATR[:, :, Q_RANK:], KV_RANK, 4)
            root(2)
            root(4)
            columns_hi(5, latT_hi, QT + VT,
                       gain=lambda k: col[:, C_QLAT + k:C_QLAT + k + 1], shift=lambda k: zero_c[:])
            for slot in range(SLOTS):
                split()
            act.wait_ge(kr_T, 1)
            nc.scalar.activation(krT, PS[0:ROPE, B_O, 0:SEQ], ACT.Copy).then_inc(kr_ready, 1)
            for _ in range(18):
                split()
            with T.loop(4, ready_landed0=32, ready_landed1=32, free_chunk_used=4) as i:
                for _ in range(4):
                    split()
            nc.scalar.preload_act_table_set("natural_log_exp_and_others")
            HEADS4 = dict(ready_qk_transposed=4, free_scores_done=4, ready_nm_full=4, ready_p_transposed=4,
                          free_p_transposed=4, free_o_ready=4)
            with T.loop(4, **SP_, **HEADS4) as i:
                for slot in range(SLOTS):
                    split()
                    if slot - 2 in START:
                        after_P("mla")
                    if slot - 1 in START:
                        after_S("mla")
                    if slot in START:
                        after_T("mla")
            T.skip(acc_ready, 4 + 3 + 1 + 9 + 8 + 4)
            T.skip(chunk_used, (4 + 3 + 1) * SLOTS + 18 + 16 + 4 * SLOTS)
            with T.loop(4, **GATED, **HEADS4) as i:
                for slot in range(SLOTS):
                    split()
                    if slot - 2 in START:
                        after_P("swa")
                    if slot - 1 in START:
                        after_S("swa", i * 4 + START.index(slot - 1))
                    if slot in START:
                        after_T("swa")
                gate(ACT.Sigmoid)
            with T.loop(4, **GATED) as i:
                for slot in range(SLOTS):
                    split()
                gate(ACT.Sigmoid)
            columns_hi(8, aT_hi, KT)
            with T.loop(4, **SP_) as i:
                for slot in range(SLOTS):
                    split()
            rms(MIX, D, 0)
            root(0)
            rms(X, D, 2)
            root(2)
            columns_hi(8, aT_hi, KT, gain=lambda k: gains[:, 1, k:k + 1], shift=lambda k: mod[:, SH2, k:k + 1])

            def conv(pair):
                b = n_pair[0] % 2
                n_pair[0] += 1
                bank = 4 * (n_pair[0] - 1 >> 1 & 1) + (n_pair[0] - 1) % 2
                if b == 0:
                    act.wait_ge(up_ready, T.ready(up_ready))
                else:
                    act.wait_ge(chunk_used, T.ready(chunk_used, SLOTS))
                act.wait_ge(up_free, T.free(up_free))
                for k, (dst, tile) in enumerate(((conv_g[b], pair), (conv_u[b], pair + FT))):
                    last = nc.scalar.activation(dst, PS[:, bank + 2 * k, 0:SEQ], ACT.Identity,
                                                bias=col[:, ds(tile + C_CONVB, 1)],
                                                scale=col[:, ds(tile + (C_CONVW + 2 * P), 1)])
                last.then_inc(conv_a, 1)
                act.wait_ge(conv_d, T.ready(conv_d))
                nc.scalar.activation(conv_g[b], conv_g[b], ACT.Silu).then_inc(conv_s, 1)

            n_pair = [0]
            T.skip(chunk_used, 4 * SLOTS)
            T.skip(up_free, 2, "free")
            with T.loop(11, ready_landed0=128, ready_landed1=128, free_chunk_used=16, ready_up_ready=2,
                        ready_chunk_used=16, free_up_free=4, ready_conv_d=4) as i:
                for j in range(2):
                    for slot in range(SLOTS):
                        split()
                    for e in range(2):
                        conv(i * 4 + (2 * j + e))

            def y_split(kt, slot):
                nc.scalar.activation(aT_hi[:, slot, :], YT[:, ds(kt, 1), :].rearrange("p a t -> p (a t)"),
                                     ACT.Copy).then_inc(y_hi, 1)

            act.wait_ge(g_ready, 1)
            y_split(0, 0)
            with T.loop(FT // 2 - 1, ready_landed0=32, ready_landed1=32, free_chunk_used=4) as i:
                for j in range(2):
                    split()
                    y_split(i * 2 + (j + 1), (j + 1) % 2)
                    split()
            split()
            y_split(FT - 1, 1)
            for s in range(ST):
                act.wait_ge(down_done, s + 1)
                nc.scalar.activation(H_FFN[:, s, :], PS[:, 4 * s:4 * s + 4, :].rearrange("p b n -> p (b n)"),
                                     ACT.Square, accum_out=stat[:, s:s + 1]).then_inc(act_step, 1)
                act.wait_ge(act_step, T.ready(act_step))
            nc.scalar.nop().then_inc(var_ready, 1)
            root(0)

        @block.vector
        def _(dve):
            T = Tally(dve, credits)
            n = [0]

            def split():
                m = n[0]
                n[0] += 1
                dve.wait_ge(hi_ready, T.ready(hi_ready))
                nc.vector.tensor_tensor(w_lo[:, m % RING, :], raw[:, m // 2 % 2, 1024 * (m % 2):1024 * (m % 2 + 1)],
                                        w_hi[:, m % RING, :].bitcast(F32), ALU.subtract).then_inc(lo_ready, 1)

            def link(ins):
                ins.then_inc(dve_step, 1)
                dve.wait_ge(dve_step, T.ready(dve_step))

            give(dve, "acc_free0", "acc_free1", "ada_done", "s_read", "o_done", "bias_used", "up_free",
                 "sb_o_done")

            def products(s, chunks=SLOTS):
                if s == 0:
                    dve.wait_ge(acc_ready, T.ready(acc_ready))
                else:
                    dve.wait_ge(chunk_used, T.ready(chunk_used, chunks))

            def gated(s):
                dve.wait_ge(gate_ready, T.ready(gate_ready))
                if s == 0:
                    T.skip(acc_ready)
                else:
                    T.skip(chunk_used, SLOTS)

            def copy_out(dst, chunks=SLOTS):
                for s in range(ST):
                    products(s, chunks)
                    d = dst(s)
                    nc.vector.tensor_copy(d, PS[:, s, 0:d.shape[-1]]).then_inc(acc_free[s], 1)

            def gate_out(dst):
                for s in range(ST):
                    gated(s)
                    nc.vector.tensor_tensor(dst(s), dst(s), PS[:, s, :], ALU.mult).then_inc(acc_free[s], 1)

            def ada(acc, half, kt):
                j = n_ada[0] % 2
                n_ada[0] += 1
                dve.wait_ge(ada_landed[j], T.ready(ada_landed[j], 16))
                part = acc[:, 1024 * half:1024 * (half + 1)]
                dve.wait_ge(ada_done, T.ready(ada_done, 0))
                nc.vector.scalar_tensor_tensor(out=part, in0=ada_raw[:, j, :], scalar=silu_c[:, ds(kt, 1)],
                                               in1=part, op0=ALU.mult, op1=ALU.add).then_inc(ada_done, 1)
                T.skip(ada_done)

            n_ada = [0]

            def mod_columns(parts):
                for part in parts:
                    dve.wait_ge(ada_cols, T.ready(ada_cols))
                    nc.vector.tensor_tensor(mod[:, part, :], PS[:, B_O, 0:KT],
                                            col[:, C_ADA + KT * part:C_ADA + KT * (part + 1)], ALU.add)\
                        .then_inc(mod_ready, 1)
                    T.skip(mod_ready)

            def rms_scale(src, dst, width, at):
                dve.wait_ge(var_ready, T.ready(var_ready))
                nc.vector.tensor_scalar(stat[:, at:at + ST], stat[:, at:at + ST], 1.0 / width, EPS,
                                        ALU.mult, ALU.add).then_inc(std_ready, 1)
                dve.wait_ge(var_ready, T.ready(var_ready))
                link(nc.vector.reciprocal(stat[:, at:at + ST], stat[:, at:at + ST]))
                if dst is not None:
                    for s in range(ST):
                        nc.vector.tensor_scalar(dst[:, s, 0:width], src[:, s, 0:width],
                                                stat[:, at + s:at + s + 1], None, ALU.mult).then_inc(rows_ready, 1)

            def columns_lo(groups, dst, hi, gain=None, shift=None):
                for j in range(groups):
                    dve.wait_ge(aT_hi_ready, T.ready(aT_hi_ready))
                    bank = PS[:, B_T + j % 4, :]
                    if gain is not None:
                        dve.wait_ge(aT_ready, T.ready(aT_ready, 0))
                        for k in range(2):
                            last = nc.vector.tensor_scalar(full[:, SEQ * k:SEQ * (k + 1)], bank[:, SEQ * k:SEQ * (k + 1)],
                                                           gain(2 * j + k), shift(2 * j + k), ALU.mult, ALU.add)
                        link(last)
                        bank = full
                    nc.vector.tensor_tensor(dst[:, 2 * j:2 * j + 2, :].rearrange("p k t -> p (k t)"), bank,
                                            hi[:, 2 * j:2 * j + 2, :].rearrange("p k t -> p (k t)").bitcast(F32),
                                            ALU.subtract).then_inc(aT_ready, 1)
                    T.skip(aT_ready)

            full = s_sb[:, :, :].rearrange("p a b -> p (a b)")[:, 0:512]

            def descending(at, n):
                whole = bias[:, :]
                return bass.AP(whole.tensor, whole.offset + at + n - 1, [list(whole.ap[0]), [-1, n]])

            def softmax(kind, scale, pair=None, mask_slot=None):
                dve.wait_ge(scores_done, T.ready(scores_done))
                dve.wait_ge(p_transposed, T.free(p_transposed))
                if kind == "b":
                    dve.wait_ge(bias_landed[mask_slot], T.ready(bias_landed[mask_slot], 64))
                    at = [(384 * mask_slot, 384 * mask_slot + P)]
                    back = True
                elif kind == "swa":
                    dve.wait_ge(bias_landed[mask_slot], T.ready(bias_landed[mask_slot], 32))
                    at = [(512 * mask_slot + BAND * e, 512 * mask_slot + BAND * e) for e in range(2)]
                    back = True
                else:
                    at = [(0, P)]
                    back = False
                heads = range(len(at))
                for e in heads:
                    for t, (a, b) in enumerate(((0, P), (P, 384))):
                        last = nc.vector.scalar_tensor_tensor(
                            out=s_sb[:, e, a:b], in0=PS[:, B_S0 - e, a:b], scalar=scale,
                            in1=descending(at[e][t], b - a) if back else bias[:, at[e][t]:at[e][t] + b - a],
                            op0=ALU.mult, op1=ALU.add)
                last.then_inc(s_read, 1)
                dve.wait_ge(s_read, T.ready(s_read))
                for e in heads:
                    for t, (a, b) in enumerate(((0, P), (P, 384))):
                        last = nc.vector.tensor_reduce(smx[:, 2 * e + t:2 * e + t + 1], s_sb[:, e, a:b], AX.X, ALU.max)
                if kind != "mla":
                    last.then_inc(bias_used, 1)
                    dve.wait_ge(bias_used, T.ready(bias_used))
                else:
                    link(last)
                if kind == "swa":
                    for e in heads:
                        last = nc.vector.tensor_scalar(smx[:, 2 * e:2 * e + 2], smx[:, 2 * e:2 * e + 2],
                                                       sink[:, ds(pair * 2 + e, 1)], None, ALU.max)
                    link(last)
                nc.vector.tensor_scalar(smx[:, 4:8] if kind == "swa" else smx[:, 4:6],
                                        smx[:, 0:4] if kind == "swa" else smx[:, 0:2], -1.0, None, ALU.mult)\
                    .then_inc(nm_full, 1)

            def weigh(kind, b):
                wide = 4 if kind == "swa" else 2
                dve.wait_ge(p_done, T.ready(p_done))
                if kind == "swa":
                    link(nc.vector.tensor_tensor(smx[:, 16:20], smx[:, 8:12], smx[:, 12:16], ALU.add))
                    link(nc.vector.reciprocal(smx[:, 20 + 4 * b:24 + 4 * b], smx[:, 16:20]))
                else:
                    link(nc.vector.reciprocal(smx[:, 20 + 4 * b:20 + 4 * b + wide], smx[:, 8:8 + wide]))

            def heads_out(kind, b, dst):
                dve.wait_ge(o_ready, T.ready(o_ready))
                for e in range(2 if kind == "swa" else 1):
                    w = SWA_D if kind == "swa" else HD
                    for t in range(ST):
                        last = nc.vector.tensor_scalar(dst(t, e), PS[:, B_O, HD * t + w * e:HD * t + w * (e + 1)],
                                                       smx[:, 20 + 4 * b + 2 * e + t:21 + 4 * b + 2 * e + t],
                                                       None, ALU.mult)
                last.then_inc(o_done, 1)

            def stage_b(h):
                dve.wait_ge(qk_transposed, T.free(qk_transposed))
                src = QKV_B[:, :, 0:2 * N_B * HD].rearrange("p s (k n) -> p s k n", k=2)[:, :, :, ds(h * HD, HD)]
                link(nc.vector.tensor_tensor(stage[:], src, src, ALU.mult))
                link(nc.vector.tensor_reduce(stat[:, 12:16].rearrange("p (s k) -> p s k", s=ST), stage[:], AX.X, ALU.add))
                nc.vector.tensor_scalar(stat[:, 8:12], stat[:, 12:16], 1.0 / HD, EPS, ALU.mult, ALU.add)\
                    .then_inc(ss_full, 1)
                dve.wait_ge(rs_full, T.ready(rs_full))
                r = stat[:, 8:12].rearrange("p (s k a) -> p s k a", s=ST, k=2).to_broadcast([P, ST, 2, HD])
                nc.vector.tensor_tensor(stage[:], src, r, ALU.mult).then_inc(stage_full, 1)

            def sb_P(b):
                dve.wait_ge(sb_ln, T.ready(sb_ln))
                for e, w in ((0, SEQ), (1, P)):
                    last = nc.vector.scalar_tensor_tensor(out=s_sb[:, e, 0:w], in0=PS[:, B_Z[b][e], 0:w], scalar=0.0,
                                                          in1=s_sb[:, e, 0:w], op0=ALU.max, op1=ALU.add)
                link(last)
                for e in range(2):
                    last = nc.vector.tensor_tensor(s_sb[:, e, 0:P], s_sb[:, e, 0:P], below[:], ALU.mult)
                last.then_inc(sb_spdone, 1)

            def sb_out(h):
                dve.wait_ge(sb_o_ready, T.ready(sb_o_ready))
                nc.vector.tensor_copy(QKV_A[:, :, ds(h * HD, HD)],
                                      PS[:, B_O, 0:2 * HD].rearrange("p (t n) -> p t n", t=ST)).then_inc(sb_o_done, 1)

            DP = dict(**DVE_PANEL, ready_acc_ready=1, ready_chunk_used=8)
            G1 = dict(**DP, ready_ada_landed0=48, ready_ada_landed1=48, ready_ada_done=6)
            ada_order = [(0, 0), (0, 1), (1, 0), (1, 1), (2, 0), (2, 1)]

            dve.wait_ge(par_T, 1)
            for t, r in enumerate(PARAM_ROWS):
                last = nc.vector.tensor_copy(col[:, P * t:P * t + r], PS[:, 6 + t // 4, P * (t % 4):P * (t % 4) + r])
            last.then_inc(par_ready, 1)
            dve.wait_ge(win_cols, 1)
            nc.vector.tensor_copy(expanded, PS[0:SWA_H, B_O - 1, 0:383]).then_inc(win_ready, 1)
            dve.wait_ge(x_landed, 32)
            nc.vector.nop().then_inc(sq_ready, 1)
            rms_scale(X, H, D, 0)
            for _ in range(AHEAD):
                split()
            columns_lo(8, aT_lo, aT_hi, gain=lambda k: col[:, C_NORM + k:C_NORM + k + 1], shift=lambda k: zero_c[:])
            link(nc.vector.memset(arena[:, 12288:12288 + 3 * 2048], 0.0))
            dve.wait_ge(silu_ready, 1)

            def g1_slot(slot, kt):
                split()
                if slot < 6:
                    j, half = ada_order[slot]
                    ada(ADA_ACC[j], half, kt)

            with T.loop(6, **G1) as i:
                for slot in range(SLOTS):
                    g1_slot(slot, i)
                copy_out(lambda s: QKV_B[:, s, ds(i * PANEL, PANEL)])
            with T.loop(4, **G1, free_qk_transposed=2, ready_dve_step=6, ready_rs_full=2, ready_scores_done=2,
                        free_p_transposed=2, ready_bias_landed0=64, ready_bias_landed1=64, ready_s_read=2,
                        ready_bias_used=2, ready_p_done=2, ready_o_ready=2) as i:
                for slot in range(SLOTS):
                    g1_slot(slot, i + 6)
                    if slot - 3 in START_B:
                        b = START_B.index(slot - 3)
                        heads_out("b", b, lambda t, e: QKV_B[:, t, ds(i * (2 * HD) + b * HD, HD)])
                    if slot - 2 in START_B:
                        weigh("b", START_B.index(slot - 2))
                    if slot - 1 in START_B:
                        softmax("b", HD ** -0.5, mask_slot=START_B.index(slot - 1))
                    if slot + 1 in START_B:
                        stage_b(i * 2 + START_B.index(slot + 1))
                copy_out(lambda s: QKV_A[:, s, ds(i * PANEL, PANEL)])
            with T.loop(2, **G1) as i:
                for slot in range(SLOTS):
                    g1_slot(slot, i + 10)
                copy_out(lambda s: QKV_A[:, s, ds(i * PANEL + 2048, PANEL)])
            with T.loop(2, **G1, ready_sb_ln=4, ready_dve_step=4, ready_sb_o_ready=4, ready_gate_ready=2) as i:
                for slot in range(SLOTS):
                    g1_slot(slot, i + 12)
                    if slot - 3 in START:
                        sb_out(i * 4 + START.index(slot - 3))
                    if slot - 1 in START:
                        sb_P(START.index(slot - 1) % 2)
                gate_out(lambda s: QKV_B[:, s, ds(i * PANEL, PANEL)])
            with T.loop(2, **G1, ready_gate_ready=2) as i:
                for slot in range(SLOTS):
                    g1_slot(slot, i + 14)
                gate_out(lambda s: QKV_A[:, s, ds(i * PANEL, PANEL)])
            nc.vector.nop().then_inc(rows_ready, 2)
            columns_lo(8, aT_lo, aT_hi)
            mod_columns((SH1, SC1, SH2))
            link(nc.vector.memset(ADA_MIX, 0.0))
            OUTP = dict(**DP, ready_ada_landed0=64, ready_ada_landed1=64, ready_ada_done=8)
            dve.wait_ge(x_landed, 64)

            def add_out(c0):
                for s in range(ST):
                    products(s)
                    nc.vector.tensor_tensor(X[:, s, ds(c0, PANEL)], X[:, s, ds(c0, PANEL)], PS[:, s, :],
                                            ALU.add).then_inc(acc_free[s], 1)

            with T.loop(4, **OUTP) as i:
                for slot in range(SLOTS):
                    split()
                    ada(ADA_MIX, slot % 2, i * 4 + slot // 2)
                add_out(i * PANEL)
            dve.wait_ge(acc_free[0], T.ready(acc_free[0], 20))
            dve.wait_ge(acc_free[1], T.ready(acc_free[1], 20))
            nc.vector.nop().then_inc(sq_ready, 1)
            rms_scale(X, H, D, 0)
            mod_columns((SC2,))
            dve.wait_ge(mod_ready, T.ready(mod_ready, 0))
            for j, (g, part) in enumerate(((C_PREMIX, SC1), (C_PREFFN, SC2))):
                last = nc.vector.scalar_tensor_tensor(out=gains[:, j, :], in0=mod[:, part, :], scalar=1.0,
                                                      in1=col[:, g:g + KT], op0=ALU.add, op1=ALU.mult)
            last.then_inc(mod_ready, 1)
            dve.wait_ge(mod_ready, T.ready(mod_ready))
            columns_lo(8, aT_lo, aT_hi, gain=lambda k: gains[:, 0, k:k + 1], shift=lambda k: mod[:, SH1, k:k + 1])
            with T.loop(2, **DP) as i:
                for slot in range(SLOTS):
                    split()
                copy_out(lambda s: LATR[:, s, ds(i * PANEL, PANEL)])
            for slot in range(SLOTS):
                split()
            copy_lat = lambda s: LATR[:, s, 2 * PANEL:LAT]
            for s in range(ST):
                products(s)
                nc.vector.tensor_copy(KR[:, s, :], PS[:, s, LAT - 2 * PANEL - ROPE:LAT - 2 * PANEL])
                nc.vector.tensor_copy(copy_lat(s), PS[:, s, 0:LAT - 2 * PANEL]).then_inc(acc_free[s], 1)
            dve.wait_ge(acc_free[0], T.ready(acc_free[0], 3))
            dve.wait_ge(acc_free[1], T.ready(acc_free[1], 3))
            nc.vector.nop().then_inc(sq_ready, 2)
            dve.wait_ge(var_ready, T.ready(var_ready, 2))
            for at, width in ((2, Q_RANK), (4, KV_RANK)):
                nc.vector.tensor_scalar(stat[:, at:at + ST], stat[:, at:at + ST], 1.0 / width, EPS,
                                        ALU.mult, ALU.add).then_inc(std_ready, 1)
            dve.wait_ge(var_ready, T.ready(var_ready, 2))
            link(nc.vector.reciprocal(stat[:, 2:6], stat[:, 2:6]))
            for s in range(ST):
                nc.vector.tensor_scalar(LATN[:, s, 0:Q_RANK], LATR[:, s, 0:Q_RANK], stat[:, 2 + s:3 + s], None, ALU.mult)
                nc.vector.tensor_scalar(LATN[:, s, Q_RANK:LAT - ROPE], LATR[:, s, Q_RANK:LAT - ROPE],
                                        stat[:, 4 + s:5 + s], None, ALU.mult).then_inc(rows_ready, 1)
            columns_lo(5, latT_lo, latT_hi, gain=lambda k: col[:, C_QLAT + k:C_QLAT + k + 1], shift=lambda k: zero_c[:])
            for slot in range(SLOTS):
                split()
            copy_out(lambda s: KVS[:, s, :])
            dve.wait_ge(x_saved, 32)
            for c in range(3):
                for _ in range(6):
                    split()
                for half in range(2):
                    for s in range(ST):
                        products(s if half else 0, QT)
                        nc.vector.tensor_copy(Q[:, s, 1024 * c + PANEL * half:1024 * c + PANEL * (half + 1)],
                                              PS[:, 2 * half + s, :]).then_inc(acc_free[s], 1)
            with T.loop(4, ready_hi_ready=4, ready_acc_ready=2, ready_chunk_used=4) as i:
                for j in range(2):
                    split()
                    split()
                    copy_out(lambda s: KV[:, s, ds(i * 1024 + PANEL * j, PANEL)], VT // 2)
            dve.wait_ge(mask_ready, 2)
            HEADS4 = dict(ready_scores_done=4, free_p_transposed=4, ready_s_read=4, ready_p_done=4, ready_o_ready=4)
            with T.loop(4, **DP, **HEADS4, ready_dve_step=8) as i:
                for slot in range(SLOTS):
                    split()
                    if slot - 3 in START:
                        j = START.index(slot - 3)
                        heads_out("mla", j % 2, lambda t, e: Q[:, t, ds(i * (4 * (HD + ROPE)) + j * (HD + ROPE), HD)])
                    if slot - 2 in START:
                        weigh("mla", START.index(slot - 2) % 2)
                    if slot - 1 in START:
                        softmax("mla", float((HD + ROPE) ** -0.5))
                copy_out(lambda s: QS[:, s, ds(i * PANEL, PANEL)])
            def QO(s, p):
                return Q[:, s, ds(p * (4 * (HD + ROPE)), 4 * (HD + ROPE))].rearrange("p (h n) -> p h n", h=4)[:, :, 0:HD]

            def gate_mla(p):
                for s in range(ST):
                    gated(s)
                    o = QO(s, p)
                    nc.vector.tensor_tensor(o, o, PS[:, s, :].rearrange("p (h n) -> p h n", h=4), ALU.mult)\
                        .then_inc(acc_free[s], 1)

            with T.loop(4, **DP, **HEADS4, ready_bias_landed0=64, ready_bias_landed1=64, ready_bias_used=4,
                        ready_gate_ready=2, ready_dve_step=12) as i:
                for slot in range(SLOTS):
                    split()
                    if slot - 3 in START:
                        j = START.index(slot - 3)
                        heads_out("swa", j % 2, lambda t, e: QS[:, t, ds(i * PANEL + (P * j + SWA_D * e), SWA_D)])
                    if slot - 2 in START:
                        weigh("swa", START.index(slot - 2) % 2)
                    if slot - 1 in START:
                        j = START.index(slot - 1)
                        softmax("swa", SWA_D ** -0.5, i * 4 + j, j % 2)
                gate_mla(i)
            with T.loop(4, **DP, ready_gate_ready=2, ready_dve_step=2) as i:
                for slot in range(SLOTS):
                    split()
                for s in range(ST):
                    gated(s)
                    o = QS[:, s, ds(i * PANEL, PANEL)]
                    link(nc.vector.tensor_tensor(o, o, PS[:, s, :], ALU.mult))
                    o = o.rearrange("p (h n) -> p h n", h=4)
                    nc.vector.tensor_tensor(o, o, QO(s, i), ALU.add).then_inc(acc_free[s], 1)
            nc.vector.nop().then_inc(rows_ready, 2)
            columns_lo(8, aT_lo, aT_hi)
            link(nc.vector.memset(ADA_MIX, 0.0))
            with T.loop(4, **OUTP) as i:
                for slot in range(SLOTS):
                    split()
                    ada(ADA_MIX, slot % 2, i * 4 + slot // 2)
                copy_out(lambda s: MIX[:, s, ds(i * PANEL, PANEL)])

            for s in range(ST):
                dve.wait_ge(acc_free[s], 1 + N_PANELS)
            nc.vector.nop().then_inc(sq_ready, 1)
            rms_scale(MIX, None, D, 0)
            mod_columns((GT1,))
            dve.wait_ge(mod_ready, T.ready(mod_ready, 0))
            link(nc.vector.tensor_tensor(gains[:, 2, :], mod[:, GT1, :], col[:, C_POSTMIX:C_POSTMIX + KT], ALU.mult))

            def diagonals():
                for b in range(4):
                    if b >= 2:
                        dve.wait_ge(diag_used, T.ready(diag_used))
                    for k in range(4):
                        last = nc.vector.tensor_scalar(diag[:, b % 2, P * k:P * (k + 1)], ident[:],
                                                       gains[:, 2, 4 * b + k:4 * b + k + 1], None, ALU.mult)
                    last.then_inc(diag_ready, 1)
                dve.wait_ge(diag_used, T.ready(diag_used, 2))

            def g_copy(dst):
                link(nc.vector.tensor_copy(dst, PS[:, B_T:B_T + 4, :].rearrange("p b n -> p (b n)")))

            diagonals()
            g_copy(G_MIX)
            dve.wait_ge(x_landed, 96)
            for s in range(ST):
                link(nc.vector.scalar_tensor_tensor(out=MIX[:, s, :], in0=MIX[:, s, :], scalar=stat[:, s:s + 1],
                                                    in1=G_MIX, op0=ALU.mult, op1=ALU.mult))
                link(nc.vector.tensor_tensor(X[:, s, :], X[:, s, :], MIX[:, s, :], ALU.add))
            nc.vector.nop().then_inc(sq_ready, 1)
            rms_scale(X, H_FFN, D, 2)
            columns_lo(8, aT_lo, aT_hi, gain=lambda k: gains[:, 1, k:k + 1], shift=lambda k: mod[:, SH2, k:k + 1])
            link(nc.vector.memset(ADA_FFN, 0.0))

            def conv(pair):
                b = n_pair[0] % 2
                bank = 4 * (n_pair[0] >> 1 & 1) + n_pair[0] % 2
                n_pair[0] += 1
                dve.wait_ge(conv_a, T.ready(conv_a))
                for tap, shift in ((1, 1), (0, 2)):
                    for k, (dst, tile) in enumerate(((conv_g[b], pair), (conv_u[b], pair + FT))):
                        last = nc.vector.scalar_tensor_tensor(
                            out=dst[:, shift:SEQ], in0=PS[:, bank + 2 * k, 0:SEQ - shift],
                            scalar=col[:, ds(tile + (C_CONVW + P * tap), 1)], in1=dst[:, shift:SEQ],
                            op0=ALU.mult, op1=ALU.add)
                    if tap:
                        link(last)
                last.then_inc(conv_d, 1)
                dve.wait_ge(conv_s, T.ready(conv_s))
                nc.vector.tensor_tensor(YT[:, ds(pair, 1), :].rearrange("p a t -> p (a t)"), conv_g[b], conv_u[b],
                                        ALU.mult).then_inc(up_free, 1)

            n_pair = [0]
            UP = dict(ready_hi_ready=16, ready_conv_a=4, ready_dve_step=4, ready_conv_s=4)
            with T.loop(8, **UP, ready_ada_landed0=32, ready_ada_landed1=32, ready_ada_done=4) as i:
                for j in range(2):
                    for slot in range(SLOTS):
                        split()
                        if slot < 2:
                            ada(ADA_FFN, slot, i * 2 + j)
                    for e in range(2):
                        conv(i * 4 + (2 * j + e))
            with T.loop(3, **UP) as i:
                for j in range(2):
                    for slot in range(SLOTS):
                        split()
                    for e in range(2):
                        conv(i * 4 + (32 + 2 * j + e))
            mod_columns((GT2,))
            dve.wait_ge(mod_ready, T.ready(mod_ready, 0))
            link(nc.vector.tensor_tensor(gains[:, 2, :], mod[:, GT2, :], col[:, C_POSTFFN:C_POSTFFN + KT], ALU.mult))
            diagonals()
            nc.vector.tensor_copy(G_FFN, PS[:, B_T:B_T + 4, :].rearrange("p b n -> p (b n)")).then_inc(g_ready, 1)

            def y_split(kt, slot):
                dve.wait_ge(y_hi, T.ready(y_hi))
                nc.vector.tensor_tensor(aT_lo[:, slot, :], YT[:, ds(kt, 1), :].rearrange("p a t -> p (a t)"),
                                        aT_hi[:, slot, :].bitcast(F32), ALU.subtract).then_inc(y_ready, 1)

            dve.wait_ge(up_free, T.ready(up_free, 2 * 22))
            y_split(0, 0)
            with T.loop(FT // 2 - 1, ready_hi_ready=4, ready_y_hi=2) as i:
                for j in range(2):
                    split()
                    y_split(i * 2 + (j + 1), (j + 1) % 2)
                    split()
            split()
            y_split(FT - 1, 1)
            dve.wait_ge(down_done, 2)
            dve.wait_ge(var_ready, T.ready(var_ready))
            nc.vector.tensor_scalar(stat[:, 0:ST], stat[:, 0:ST], 1.0 / D, EPS, ALU.mult, ALU.add).then_inc(std_ready, 1)
            dve.wait_ge(var_ready, T.ready(var_ready))
            link(nc.vector.reciprocal(stat[:, 0:ST], stat[:, 0:ST]))
            for s in range(ST):
                link(nc.vector.scalar_tensor_tensor(out=H_FFN[:, s, :],
                                                    in0=PS[:, 4 * s:4 * s + 4, :].rearrange("p b n -> p (b n)"),
                                                    scalar=stat[:, s:s + 1], in1=G_FFN, op0=ALU.mult, op1=ALU.mult))
                nc.vector.tensor_tensor(X[:, s, :], X[:, s, :], H_FFN[:, s, :], ALU.add).then_inc(fin_ready, 1)

        @block.tensor
        def _(pe):
            T = Tally(pe, credits)
            n = [0]
            give(pe, "chunk_used", "qk_transposed", "scores_done", "p_transposed", "o_ready", "sb_transposed",
                 "sb_zdone", "sb_cum", "sb_o_ready")

            def three(dst, a_hi, a_lo, w_h, w_l, first, last, weights_first=False):
                if weights_first:
                    passes = ((w_h, a_hi), (w_h, a_lo), (w_l, a_hi))
                else:
                    passes = ((a_hi, w_h), (a_hi, w_l), (a_lo, w_h))
                for j, (l, r) in enumerate(passes):
                    mm = pe.matmul(dst, l, r, start=first and j == 0, stop=last and j == 2)
                return mm

            def chunk(slot, kts, a_hi=None, a_lo=None, width=PANEL, k0=0):
                a_hi, a_lo = a_hi or aT_hi, a_lo or aT_lo
                m = n[0] % RING
                n[0] += 1
                pe.wait_ge(lo_ready, T.ready(lo_ready))
                wh = w_hi[:, m, :].rearrange("p (k n) -> p k n", k=2)
                wl = w_lo[:, m, :].rearrange("p (k n) -> p k n", k=2)
                for s in range(ST):
                    if slot == 0:
                        pe.wait_ge(acc_free[s], T.free(acc_free[s]))
                    for k in range(2):
                        kt = 2 * slot + k
                        mm = three(PS[:, s, 0:width], a_hi[:, k0 + kt, s * P:(s + 1) * P], a_lo[:, k0 + kt, s * P:(s + 1) * P],
                                   wh[:, k, 0:width], wl[:, k, 0:width], kt == 0, kt == kts - 1)
                    if slot == kts // 2 - 1 and s == 0:
                        mm.then_inc(acc_ready, 1)
                mm.then_inc(chunk_used, 1)

            def transpose_rows(src, groups, ready=2):
                pe.wait_ge(rows_ready, T.ready(rows_ready, ready))
                for j in range(groups):
                    if j >= 4:
                        pe.wait_ge(aT_ready, T.ready(aT_ready, 0) + j - 3)
                    for k in range(2):
                        for s in range(ST):
                            tr = pe.transpose(PS[:, B_T + j % 4, SEQ * k + P * s:SEQ * k + P * (s + 1)],
                                              src(s, 2 * j + k), ident[:])
                    tr.then_inc(rows_T, 1)
                pe.wait_ge(aT_ready, T.ready(aT_ready, groups))

            def ada_reduce(acc):
                for k in range(KT):
                    mm = pe.matmul(PS[:, B_O, k:k + 1], acc[:, P * k:P * (k + 1)], ones[:, 0:1], start=True, stop=True)
                mm.then_inc(ada_cols, 1)

            def head_T(kind):
                pe.wait_ge(stage_full, T.ready(stage_full))
                pe.wait_ge(qkT_full, T.free(qkT_full))
                for qk in range(2):
                    for s in range(ST):
                        tr = pe.transpose(PS[:, B_T, SEQ * qk + P * s:SEQ * qk + P * (s + 1)], stage[:, s, qk, :], ident[:])
                if kind == "mla":
                    for s in range(ST):
                        tr = pe.transpose(PS[0:ROPE, B_S1, P * s:P * (s + 1)], stage_r[:, s, :], ident[:])
                tr.then_inc(qk_transposed, 1)

            def head_S(kind):
                pe.wait_ge(qkT_full, T.ready(qkT_full))
                pe.wait_ge(s_read, T.free(s_read))
                for e in range(2 if kind == "swa" else 1):
                    p0, p1 = (SWA_D * e, SWA_D * (e + 1)) if kind == "swa" else (0, P)
                    for t in range(ST):
                        dst = PS[:, B_S0 - e, P * t:P * t + P * (t + 1)]
                        mm = pe.matmul(dst, qkT[p0:p1, P * t:P * (t + 1)], qkT[p0:p1, SEQ:SEQ + P * (t + 1)],
                                       start=True, stop=kind != "mla")
                        if kind == "mla":
                            mm = pe.matmul(dst, qrT[:, P * t:P * (t + 1)], krT[:, 0:P * (t + 1)], start=False, stop=True)
                mm.then_inc(scores_done, 1)

            def head_P(kind):
                pe.wait_ge(p_done, T.ready(p_done))
                pe.wait_ge(pT_full, T.free(pT_full))
                for e in range(2 if kind == "swa" else 1):
                    for b in range(3):
                        tr = pe.transpose(PS[:, B_P + e, P * b:P * (b + 1)], s_sb[:, e, P * b:P * (b + 1)], ident[:])
                tr.then_inc(p_transposed, 1)

            def head_O(kind, v, heads=1, w=HD):
                pe.wait_ge(pT_full, T.ready(pT_full))
                pe.wait_ge(o_done, T.free(o_done))
                for e in range(heads):
                    pe.matmul(PS[:, B_O, w * e:w * (e + 1)], pT[:, e, 0:P], v(0), start=True, stop=True)
                    dst = PS[:, B_O, HD + w * e:HD + w * (e + 1)]
                    pe.matmul(dst, pT[:, e, P:2 * P], v(0), start=True, stop=False)
                    mm = pe.matmul(dst, pT[:, e, 2 * P:3 * P], v(1), start=False, stop=True)
                mm.then_inc(o_ready, 1)

            def sb_T():
                pe.wait_ge(sb_staged, T.ready(sb_staged))
                pe.wait_ge(sb_qkT, T.free(sb_qkT))
                for qk in range(2):
                    for s in range(ST):
                        tr = pe.transpose(PS[:, B_T, SEQ * qk + P * s:SEQ * qk + P * (s + 1)], stage[:, s, qk, :], ident[:])
                tr.then_inc(sb_transposed, 1)

            def sb_Z(b):
                pe.wait_ge(sb_qkT, T.ready(sb_qkT))
                pe.wait_ge(sb_w_done, T.free(sb_w_done))
                pe.matmul(PS[:, B_Z[b][0], 0:SEQ], qkT[:, SEQ:SEQ + P], qkT[:, 0:SEQ], start=True, stop=False,
                          skip_group_check=True)
                pe.matmul(PS[:, B_Z[b][1], 0:P], qkT[:, SEQ + P:], qkT[:, P:SEQ], start=True, stop=False,
                          skip_group_check=True).then_inc(sb_zdone, 1)

            def sb_C(b):
                pe.wait_ge(sb_spdone, T.ready(sb_spdone))
                z0, z1 = PS[:, B_Z[b][0], 0:SEQ], PS[:, B_Z[b][1], 0:P]
                on_top = dict(start=False, skip_group_check=True)
                pe.matmul(z0, tri[:], s_sb[:, 0, 0:SEQ], stop=False, **on_top)
                pe.matmul(z0[:, P:], minus1[:], s_sb[:, 1, 0:P], stop=False, **on_top)
                pe.matmul(z0[:, 0:P], ident_b[:], neg_b[:], stop=True, **on_top)
                pe.matmul(z1, tri[:], s_sb[:, 1, 0:P], stop=False, **on_top)
                pe.matmul(z1, ident_b[:], neg_b[:], stop=True, **on_top).then_inc(sb_cum, 1)

            def sb_O(h):
                pe.wait_ge(sb_w_done, T.ready(sb_w_done))
                pe.wait_ge(sb_o_done, T.free(sb_o_done))
                v = lambda s: QKV_A[:, s, ds(h * HD + 2 * N_A * HD, HD)]
                pe.matmul(PS[:, B_O, 0:HD], pT[:, 0, 0:P], v(0), start=True, stop=True)
                pe.matmul(PS[:, B_O, HD:2 * HD], pT[:, 0, P:SEQ], v(0), start=True, stop=False)
                pe.matmul(PS[:, B_O, HD:2 * HD], pT[:, 1, 0:P], v(1), start=False, stop=True).then_inc(sb_o_ready, 1)

            pe.wait_ge(const_ready, 1)
            pe.wait_ge(par_landed, 16 * 15)
            for t, r in enumerate(PARAM_ROWS):
                tr = pe.transpose(PS[:, 6 + t // 4, P * (t % 4):P * (t % 4) + r], PARAM[0:r, t, :], ident[0:r, 0:r])
            tr.then_inc(par_T, 1)
            pe.wait_ge(par_ready, 1)
            pe.wait_ge(misc_landed, 48)
            pe.matmul(PS[0:SWA_H, B_O - 1, 0:383], table, hot, start=True, stop=True).then_inc(win_cols, 1)
            transpose_rows(lambda s, k: H[:, s, P * k:P * (k + 1)], 8)
            with T.loop(6, **PE_PANEL) as i:
                for slot in range(SLOTS):
                    chunk(slot, KT)
            with T.loop(4, **PE_PANEL, ready_stage_full=2, free_qkT_full=2, ready_qkT_full=2, free_s_read=2,
                        ready_p_done=2, free_pT_full=2, ready_pT_full=2, free_o_done=2) as i:
                for slot in range(SLOTS):
                    chunk(slot, KT)
                    if slot - 3 in START_B:
                        j = START_B.index(slot - 3)
                        head_O("b", lambda s: QKV_B[:, s, ds(i * (2 * HD) + (j + 2 * N_B) * HD, HD)])
                    if slot - 2 in START_B:
                        head_P("b")
                    if slot - 1 in START_B:
                        head_S("b")
                    if slot in START_B:
                        head_T("b")
            with T.loop(2, **PE_PANEL) as i:
                for slot in range(SLOTS):
                    chunk(slot, KT)
            pe.wait_ge(o_done, credits["o_done"] + N_B)
            with T.loop(2, **PE_PANEL, ready_sb_staged=4, free_sb_qkT=4, ready_sb_qkT=4, free_sb_w_done=4,
                        ready_sb_spdone=4, ready_sb_w_done=4, free_sb_o_done=4) as i:
                for slot in range(SLOTS):
                    chunk(slot, KT)
                    if slot - 3 in START:
                        sb_O(i * 4 + START.index(slot - 3))
                    if slot - 2 in START:
                        sb_C(START.index(slot - 2) % 2)
                    if slot - 1 in START:
                        sb_Z(START.index(slot - 1) % 2)
                    if slot in START:
                        sb_T()
            with T.loop(2, **PE_PANEL) as i:
                for slot in range(SLOTS):
                    chunk(slot, KT)
            pe.wait_ge(acc_free[0], 1 + 16)
            pe.wait_ge(acc_free[1], 1 + 16)
            transpose_rows(lambda s, k: (QKV_A if k < 8 else QKV_B)[:, s, P * (k % 8):P * (k % 8 + 1)], 8)
            pe.wait_ge(ada_done, credits["ada_done"] + 96)
            for j in range(3):
                if j:
                    pe.wait_ge(mod_ready, j)
                ada_reduce(ADA_ACC[j])
            with T.loop(4, **PE_PANEL) as i:
                for slot in range(SLOTS):
                    chunk(slot, KT)
            pe.wait_ge(ada_done, credits["ada_done"] + 96 + 32)
            pe.wait_ge(mod_ready, 3)
            ada_reduce(ADA_MIX)
            transpose_rows(lambda s, k: H[:, s, P * k:P * (k + 1)], 8)
            with T.loop(2, **PE_PANEL) as i:
                for slot in range(SLOTS):
                    chunk(slot, KT)
            for slot in range(SLOTS):
                chunk(slot, KT, width=LAT - 2 * PANEL)
            transpose_rows(lambda s, k: LATN[:, s, P * k:P * (k + 1)], 5)
            for slot in range(SLOTS):
                chunk(slot, KT)
            pe.wait_ge(kr_staged, 1)
            for s in range(ST):
                tr = pe.transpose(PS[0:ROPE, B_O, P * s:P * (s + 1)], stage_r[:, s, :], ident[:])
            tr.then_inc(kr_T, 1)
            pe.wait_ge(kr_ready, 1)
            for c in range(3):
                for kt in range(QT):
                    m = n[0] % RING
                    n[0] += 1
                    pe.wait_ge(lo_ready, T.ready(lo_ready))
                    for half in range(2):
                        for s in range(ST):
                            if kt == 0 and half == 0:
                                pe.wait_ge(acc_free[s], T.free(acc_free[s], 2 if c else 1))
                            cols = slice(PANEL * half, PANEL * (half + 1))
                            mm = three(PS[:, 2 * half + s, :], latT_hi[:, kt, s * P:(s + 1) * P],
                                       latT_lo[:, kt, s * P:(s + 1) * P], w_hi[:, m, cols], w_lo[:, m, cols],
                                       kt == 0, kt == QT - 1)
                            if kt == QT - 1 and (half, s) != (1, 1):
                                mm.then_inc(acc_ready, 1)
                    mm.then_inc(chunk_used, 1)
            for s in range(ST):
                T.skip(acc_free[s], 1, "free")
            with T.loop(4, ready_lo_ready=4, free_acc_free0=2, free_acc_free1=2) as i:
                for j in range(2):
                    for slot in range(2):
                        chunk(slot, VT, latT_hi, latT_lo, k0=QT)
            HEADS4 = dict(ready_stage_full=4, free_qkT_full=4, ready_qkT_full=4, free_s_read=4,
                          ready_p_done=4, free_pT_full=4, ready_pT_full=4, free_o_done=4)
            with T.loop(4, **PE_PANEL, **HEADS4) as i:
                for slot in range(SLOTS):
                    chunk(slot, KT)
                    if slot - 3 in START:
                        j = START.index(slot - 3)
                        head_O("mla", lambda s: KV[:, s, ds(i * (8 * HD) + (2 * j + 1) * HD, HD)])
                    if slot - 2 in START:
                        head_P("mla")
                    if slot - 1 in START:
                        head_S("mla")
                    if slot in START:
                        head_T("mla")
            with T.loop(4, **PE_PANEL, **HEADS4) as i:
                for slot in range(SLOTS):
                    chunk(slot, KT)
                    if slot - 3 in START:
                        head_O("swa", lambda s: KVS[:, s, ds(i * SWA_D + SWA_G * SWA_D, SWA_D)], 2, SWA_D)
                    if slot - 2 in START:
                        head_P("swa")
                    if slot - 1 in START:
                        head_S("swa")
                    if slot in START:
                        head_T("swa")
            with T.loop(4, **PE_PANEL) as i:
                for slot in range(SLOTS):
                    chunk(slot, KT)
            transpose_rows(lambda s, k: QS[:, s, P * k:P * (k + 1)], 8)
            with T.loop(4, **PE_PANEL) as i:
                for slot in range(SLOTS):
                    chunk(slot, KT)
            pe.wait_ge(ada_done, credits["ada_done"] + 96 + 64)
            ada_reduce(ADA_MIX)

            def spread():
                for b in range(4):
                    pe.wait_ge(diag_ready, T.ready(diag_ready))
                    pe.matmul(PS[:, B_T + b, :], ones[:], diag[:, b % 2, :], start=True, stop=True)\
                      .then_inc(diag_used, 1)

            spread()
            transpose_rows(lambda s, k: H_FFN[:, s, P * k:P * (k + 1)], 8)
            order = (0, 2, 1, 3)
            pe.wait_ge(acc_free[0], 1 + N_PANELS)
            pe.wait_ge(acc_free[1], 1 + N_PANELS)
            with T.loop(11, ready_lo_ready=16, free_up_free=4) as i:
                for j in range(2):
                    for slot in range(SLOTS):
                        m = n[0] % RING
                        n[0] += 1
                        pe.wait_ge(lo_ready, T.ready(lo_ready))
                        wh = w_hi[:, m, :].rearrange("p (k n) -> p k n", k=2)
                        wl = w_lo[:, m, :].rearrange("p (k n) -> p k n", k=2)
                        for e in order:
                            if slot == 0 and e < 2:
                                pe.wait_ge(up_free, T.free(up_free))
                            for k in range(2):
                                kt = 2 * slot + k
                                mm = three(PS[:, 4 * j + e, 0:SEQ], aT_hi[:, kt, :], aT_lo[:, kt, :],
                                           wh[:, k, P * e:P * (e + 1)], wl[:, k, P * e:P * (e + 1)],
                                           kt == 0, kt == KT - 1, weights_first=True)
                            if slot == SLOTS - 1 and e == 2:
                                mm.then_inc(up_ready, 1)
                        mm.then_inc(chunk_used, 1)
            pe.wait_ge(ada_done, credits["ada_done"] + 96 + 64 + 32)
            pe.wait_ge(up_free, credits["up_free"] + 44)
            ada_reduce(ADA_FFN)
            spread()
            pe.wait_ge(g_ready, 1)
            def down(j, first, last):
                pe.wait_ge(y_ready, T.ready(y_ready))
                for half in range(2):
                    m = n[0] % RING
                    n[0] += 1
                    pe.wait_ge(lo_ready, T.ready(lo_ready))
                    for s in range(ST):
                        for c in range(2):
                            cols = slice(PANEL * c, PANEL * (c + 1))
                            mm = three(PS[:, 4 * s + 2 * half + c, :], aT_hi[:, j, s * P:(s + 1) * P],
                                       aT_lo[:, j, s * P:(s + 1) * P], w_hi[:, m, cols], w_lo[:, m, cols], first, last)
                        if last and half == 1:
                            mm.then_inc(down_done, 1)
                    if not (last and half == 1):
                        mm.then_inc(chunk_used, 1)

            down(0, True, False)
            with T.loop(FT // 2 - 1, ready_y_ready=2, ready_lo_ready=4) as i:
                for j in range(2):
                    down((j + 1) % 2, False, False)
            down(1, False, True)


_INS = ["x", "norm_g", "w_in", "q_norm_g", "k_norm_g", "rel_bias", "w_out", "c_2", "w_ada_2", "b_ada_2", "g_pre_mix_2",
        "g_post_mix_2", "w_in_2", "g_q_lat_2", "w_uq_2", "g_kv_lat_2", "w_ukv_2", "rel_bias_2", "sinks_2", "w_o_2",
        "g_pre_ffn_2", "g_post_ffn_2", "w_up_2", "conv_w_2", "conv_b_2", "w_down_2",
        "rope_cos", "rope_sin", "bucket_hot"]


def rope_tables():
    inv = (np.float32(10000.0) ** (-np.arange(0, ROPE, 2, dtype=np.float32) / np.float32(ROPE))).astype(np.float32)
    angle = np.arange(SEQ, dtype=np.float32)[:, None] * inv[None, :]
    cos, sin = np.cos(angle).astype(np.float32), np.sin(angle).astype(np.float32)
    return np.concatenate([cos, cos], 1), np.concatenate([-sin, sin], 1)


def bucket_rows():
    hot = np.zeros((BUCKETS + 1, 383), np.float32)
    exact = BUCKETS // 2
    for m in range(383):
        dist = m - (P - 1)
        if not 0 <= dist < WINDOW:
            hot[BUCKETS, m] = 1.0
            continue
        bucket = dist
        if dist >= exact:
            bucket = exact + int(np.log(np.float32(dist) / np.float32(exact)) / np.float32(np.log(WINDOW / exact))
                                 * np.float32(BUCKETS - exact))
        hot[min(bucket, BUCKETS - 1), m] = 1.0
    return hot


def kernel(**inputs):
    import concourse.bacc as bacc
    from concourse.bass_utils import run_bass_kernel_spmd

    arrays = {k: np.ascontiguousarray(v) for k, v in inputs.items()}
    arrays["rope_cos"], arrays["rope_sin"] = rope_tables()
    arrays["bucket_hot"] = bucket_rows()
    nc = bacc.Bacc("TRN2", target_bir_lowering=False, num_devices=1)
    args = [nc.dram_tensor(f"in_{n}", arrays[n].shape, mybir.dt.from_np(arrays[n].dtype), kind="ExternalInput").ap()
            for n in _INS]
    args.append(nc.dram_tensor("out_rows", (1, SEQ, D), F32, kind="ExternalOutput").ap())
    block_kernel(nc, *args)
    r = run_bass_kernel_spmd(nc, [{f"in_{n}": arrays[n] for n in _INS}], core_ids=[0])
    return r.results[0]["out_rows"]
```

```python
from contextlib import ExitStack, contextmanager

import numpy as np

import concourse.bass as bass
from concourse import mybir

F32 = mybir.dt.float32
F32R = mybir.dt.float32r
BF16 = mybir.dt.bfloat16
ALU = mybir.AluOpType
ACT = mybir.ActivationFunctionType
AX = mybir.AxisListType
ds = bass.ds

P = 128
SEQ = 256
ST = SEQ // P
D = 2048
KT = D // P
PANEL = 512
SLOTS = KT // 2
AHEAD = 3
RING = 4
EPS = 1e-6
NEG = -1e30

HD = 128
N_A = N_B = 8
CHUNK = 64
REL_CLIP = 256
N_REL = REL_CLIP + CHUNK
MLA_H, ROPE, Q_RANK, KV_RANK = 16, 64, 768, 512
QT, VT = Q_RANK // P, KV_RANK // P
LAT = Q_RANK + KV_RANK + ROPE
SWA_H, SWA_G, SWA_D, WINDOW, BUCKETS = 32, 4, 64, 128, 32
BAND = 2 * WINDOW
FF = 5632
FT = FF // P
TOEP = 384

C_NORM, C_PREMIX, C_POSTMIX, C_PREFFN, C_POSTFFN, C_C, C_QLAT, C_KVLAT, C_QN, C_KN = (
    0, 16, 32, 48, 64, 80, 96, 102, 106, 107)
C_ADA, C_CONVB, C_CONVW = 128, 256, 384
PARAM_ROWS = [108, 96, FT * 2, FT * 2, FT * 2, FT * 2]

SH1, SC1, GT1, SH2, SC2, GT2 = range(6)


class Tally:

    def __init__(self, eng, credits):
        self.eng, self.credits = eng, credits
        self.count, self.stride, self.i = {}, None, None

    def _next(self, key, k):
        self.count[key] = self.count.get(key, 0) + k
        n = self.count[key]
        if self.i is not None and key in self.stride:
            n = self.i * self.stride[key] + n
        elif self.i is not None and k:
            raise ValueError(f"no stride for {key}")
        return n

    def ready(self, sem, k=1):
        return self._next(("ready", sem.name), k) + self.credits.get(sem.name, 0)

    def free(self, sem, k=1):
        return self._next(("free", sem.name), k)

    def skip(self, sem, k=1, what="ready"):
        self._next((what, sem.name), k)

    @contextmanager
    def loop(self, n, **strides):
        keys = {}
        for name, k in strides.items():
            what, sem = name.split("_", 1)
            keys[(what, sem)] = k
        before = dict(self.count)
        with self.eng.Fori(0, n) as i:
            self.i, self.stride = i, keys
            yield i
            self.i = None
        for key in {*self.count, *keys}:
            moved = self.count.get(key, 0) - before.get(key, 0)
            if moved != keys.get(key, 0):
                raise ValueError(f"{key}: moved {moved}, stride {keys.get(key, 0)}")
            self.count[key] = before.get(key, 0) + n * moved


def block_kernel(nc, x, norm_g, w_in, q_norm_g, k_norm_g, rel_bias, w_out, c_2, w_ada_2, b_ada_2,
                 g_pre_mix_2, g_post_mix_2, w_in_2, g_q_lat_2, w_uq_2, g_kv_lat_2, w_ukv_2,
                 rel_bias_2, sinks_2, w_o_2, g_pre_ffn_2, g_post_ffn_2, w_up_2, conv_w_2, conv_b_2,
                 w_down_2, rope_cos, rope_sin, bucket_hot, out):
    ctx = ExitStack()
    with ctx:
        def sb(name, shape, dt=F32):
            return ctx.enter_context(nc.sbuf_tensor(name, shape, dt))

        semaphores = {}
        credits = {"chunk_used": RING, "acc_free0": 1, "acc_free1": 1,
                   "ada_done": 2, "qk_transposed": 1, "qkT_full": 1, "scores_done": 1, "s_read": 1,
                   "p_transposed": 1, "pT_full": 1, "o_ready": 1, "o_done": 1,
                   "bias_used": 2, "gates_used": 1, "conv_d": 4, "y_done": 2,
                   "sb_w_done": 2, "sb_o_ready": 1, "sb_o_done": 1, "sb_transposed": 1, "sb_qkT": 1,
                   "sb_zdone": 1, "sb_cum": 1}

        def sem(name):
            s = ctx.enter_context(nc.semaphore(name))
            semaphores[name] = s
            return s

        raw = sb("raw", [P, RING, 1024])
        w_hi = sb("w_hi", [P, RING, 1024], F32R)
        w_lo = sb("w_lo", [P, RING, 1024], F32R)
        aT_hi = sb("aT_hi", [P, KT, SEQ], F32R)
        aT_lo = sb("aT_lo", [P, KT, SEQ], F32R)
        latT_hi = sb("latT_hi", [P, QT + VT, SEQ], F32R)
        latT_lo = sb("latT_lo", [P, QT + VT, SEQ], F32R)
        ada_raw = sb("ada_raw", [P, 2, 1024])
        arena = sb("arena", [P, 19584])

        def rows(at, width):
            return arena[:, at:at + ST * width].rearrange("p (s n) -> p s n", s=ST)

        X = rows(0, D)
        QKV_B = rows(0, 3 * N_B * HD)
        QKV_A = rows(6144, 3 * N_A * HD)
        ADA_1 = arena[:, 12288:12288 + 2 * D]
        ADA_SC2 = arena[:, 16384:16384 + D]
        PARAM = arena[:, 16384:16384 + 768].rearrange("p (t n) -> p t n", t=6)
        Q = rows(0, MLA_H * (HD + ROPE))
        KV = rows(6144, MLA_H * 2 * HD)
        LATR = rows(6144, LAT)
        QS = rows(14336, SWA_H * SWA_D)
        KVS = rows(18432, 2 * SWA_G * SWA_D)
        KR = rows(19456, ROPE)
        MIX = rows(4096, D)
        G_MIX = arena[:, 8192:8192 + D]
        G_FFN = arena[:, 4096:4096 + D]
        H_FFN = rows(6144, D)
        YT = arena[:, 6144:6144 + FT * SEQ].rearrange("p (f t) -> p f t", f=FT)
        B_MIX = arena[:, 4096:4096 + D]
        ADA_GT1 = arena[:, 6144:6144 + D]
        ADA_SH2 = [arena[:, at:at + D] for at in (14336, 10240)]
        ADA_GT2 = arena[:, 17408:17408 + D]

        stage = sb("stage", [P, ST, 2, HD])
        qkT = sb("qkT", [P, 2 * SEQ])
        s_sb = sb("s_sb", [P, 2, 384])
        pT = sb("pT", [P, 2, 384])
        bias = sb("bias", [P, 1024])
        cosT, sinT, stage_r, tmp_r = [bias[:, P * j:P * (j + 1)].rearrange("p (s n) -> p s n", s=ST)
                                      for j in range(3, 7)]
        krT, qrT = pT[0:ROPE, 1, 0:SEQ], s_sb[0:ROPE, 1, 0:SEQ]
        ident = sb("ident", [P, P])
        ident_b = sb("ident_b", [P, P], BF16)
        tri = sb("tri", [P, P])
        minus1 = sb("minus1", [P, P])
        below = sb("below", [P, P])
        neg_b = sb("neg_b", [P, P], BF16)
        ones = sb("ones", [P, P])
        col = sb("col", [P, 6 * P])
        mod = sb("mod", [P, 6, KT])
        silu_c = sb("silu_c", [P, KT])
        gains = sb("gains", [P, 4, KT])
        zero_c = sb("zero_c", [P, 1])
        stat = sb("stat", [P, 16])
        spare = sb("spare", [P, 1])
        QK_TILES = 2 * N_B
        mean_b = sb("mean_b", [P, ST, QK_TILES])
        inv_b = sb("inv_b", [P, ST, QK_TILES])
        tmp_b = sb("tmp_b", [P, ST, QK_TILES])
        GATES = (rows(18432, PANEL), rows(12288, PANEL))
        squares = sb("squares", [P, 4 * ST])
        smx = sb("smx", [P, 28])
        sink = sb("sink", [P, SWA_H])
        minus_sink = sb("minus_sink", [P, ST, SWA_H])
        PS = ctx.enter_context(nc.psum_tensor("PS", [P, 8, 512], F32))
        B_T, B_S0, B_S1, B_P, B_O = 2, 3, 4, 5, 7
        B_G = 6
        B_UP1 = 4
        B_Z = ((4, 3), (6, 5))

        table = qkT[0:BUCKETS + 1, 0:SWA_H]
        hot = pT[0:BUCKETS + 1, 0, 0:383]
        expanded = pT[0:SWA_H, 1, 0:383]
        conv_g = [s_sb[:, 0, 0:SEQ], pT[:, 0, 0:SEQ]]
        conv_u = [s_sb[:, 1, 0:SEQ], pT[:, 1, 0:SEQ]]
        diag = stage[:, :, :, :].rearrange("p a b n -> p (a b) n")
        full = s_sb[:, :, :].rearrange("p a b -> p (a b)")[:, 0:512]

        x1_dram = nc.dram_tensor("x1_rows", (SEQ, D), F32, kind="Internal").ap()
        win_dram = nc.dram_tensor("window_bias", (SWA_H, TOEP), F32, kind="Internal").ap()

        landed = [sem(f"landed{i}") for i in range(RING)]
        hi_ready, lo_ready = sem("hi_ready"), sem("lo_ready")
        chunk_used = sem("chunk_used")
        acc_ready = sem("acc_ready")
        acc_free = [sem("acc_free0"), sem("acc_free1")]
        gate_ready = sem("gate_ready")
        gates_used = sem("gates_used")
        ada_landed = [sem("ada_landed0"), sem("ada_landed1")]
        ada_done = sem("ada_done")
        x_landed, par_landed, misc_landed = sem("x_landed"), sem("par_landed"), sem("misc_landed")
        x_again, rope_landed = sem("x_again"), sem("rope_landed")
        bias_landed = [sem("bias_landed0"), sem("bias_landed1")]
        bias_used = sem("bias_used")
        stored = sem("stored")
        const_ready = sem("const_ready")
        mask_ready = sem("mask_ready")
        par_T, par_ready = sem("par_T"), sem("par_ready")
        silu_ready = sem("silu_ready")
        act_step, dve_step, pool_step = sem("act_step"), sem("dve_step"), sem("pool_step")
        var_ready, std_ready = sem("var_ready"), sem("std_ready")
        x2_ready = sem("x2_ready")
        rows_ready = sem("rows_ready")
        rows_T = sem("rows_T")
        aT_hi_ready, aT_ready = sem("aT_hi_ready"), sem("aT_ready")
        stage_full, qk_transposed, qkT_full = sem("stage_full"), sem("qk_transposed"), sem("qkT_full")
        scores_done, s_read, nm_full = sem("scores_done"), sem("s_read"), sem("nm_full")
        p_done, p_transposed, pT_full = sem("p_done"), sem("p_transposed"), sem("pT_full")
        o_ready, o_done = sem("o_ready"), sem("o_done")
        sums_b_ready, mean_b_ready, inv_b_ready = sem("sums_b_ready"), sem("mean_b_ready"), sem("inv_b_ready")
        sb_staged, sb_transposed, sb_qkT = sem("sb_staged"), sem("sb_transposed"), sem("sb_qkT")
        sb_zdone, sb_ln, sb_spdone, sb_cum = sem("sb_zdone"), sem("sb_ln"), sem("sb_spdone"), sem("sb_cum")
        sb_w_done, sb_o_ready, sb_o_done = sem("sb_w_done"), sem("sb_o_ready"), sem("sb_o_done")
        ada_cols, mod_ready = sem("ada_cols"), sem("mod_ready")
        win_cols, win_ready, win_stored = sem("win_cols"), sem("win_ready"), sem("win_stored")
        x_saved = sem("x_saved")
        kr_staged, kr_T, kr_ready = sem("kr_staged"), sem("kr_T"), sem("kr_ready")
        acc_zeroed, row_landed, ffn_row_landed = sem("acc_zeroed"), sem("row_landed"), sem("ffn_row_landed")
        spread_done, g_read, g_copied = sem("spread_done"), sem("g_read"), sem("g_copied")
        conv_a, conv_d, conv_s, y_done = sem("conv_a"), sem("conv_d"), sem("conv_s"), sem("y_done")
        y_hi, y_ready = sem("y_hi"), sem("y_ready")
        down_done, y_scaled, fin_ready, last_ready = (
            sem("down_done"), sem("y_scaled"), sem("fin_ready"), sem("last_ready"))

        def give(eng, *names):
            for name in names:
                eng.nop().then_inc(semaphores[name], credits[name])

        block = ctx.enter_context(nc.Block())
        PE_PANEL = dict(ready_lo_ready=8, free_acc_free0=1, free_acc_free1=1)
        LANDED = {f"ready_landed{r}": 16 for r in range(RING)}
        ACT_PANEL = dict(**{k: 2 * v for k, v in LANDED.items()}, free_chunk_used=8)
        DVE_PANEL = dict(ready_hi_ready=8)
        START_B = (1, 3)

        COLUMNS = ((0, 1), (2, 3), (4,), (5,), (6,), (7,), (), ())

        def due(slot, after, start, before):
            j, odd = divmod(slot - after, 2)
            who = start if j >= 0 else before
            return None if odd or who is None else (*who, j % 4)

        N_PANELS = 16 + 4 + 3 + 1 + 6 + 8 + 4 + 4 + 4 + 4

        @block.sync
        def _(sp):
            T = Tally(sp, credits)
            n_raw, n_ada, n_bias = [0], [0], [0]

            def load(src, first=False):
                m = n_raw[0]
                n_raw[0] += 1
                if not first:
                    sp.wait_ge(lo_ready, T.ready(lo_ready))
                dst = raw[:, m % RING, :]
                if len(src.shape) == 3:
                    dst = dst.rearrange("p (k n) -> p k n", k=src.shape[1])
                sp.dma_start(dst, src).then_inc(landed[m % RING], 16)

            def load_chunk(w, j, c0, first=False):
                load(w[2 * P * j:2 * P * (j + 1), ds(c0, PANEL)].rearrange("(k p) n -> p k n", p=P), first)

            def load_ada(row, c0):
                j = n_ada[0] % 2
                n_ada[0] += 1
                sp.wait_ge(ada_done, T.free(ada_done))
                sp.dma_start(ada_raw[:, j, :], w_ada_2[0, ds(row, P), c0:c0 + 1024]).then_inc(ada_landed[j], 16)

            def panel(w, c0, following, beside=None):
                for slot in range(SLOTS):
                    if slot + RING < SLOTS:
                        load_chunk(w, slot + RING, c0)
                    else:
                        following(slot + RING - SLOTS)
                    if beside is not None:
                        beside(slot)

            def panels(n, w, c0, following, beside=None, **strides):
                strides = dict(ready_lo_ready=8, **strides)
                if n > 1:
                    with T.loop(n - 1, **strides) as i:
                        panel(w, i * PANEL + c0, lambda j: load_chunk(w, j, i * PANEL + (c0 + PANEL)),
                              None if beside is None else lambda slot: beside(i, slot))
                last = c0 + PANEL * (n - 1)
                panel(w, last, following, None if beside is None else lambda slot: beside(n - 1, slot))

            def upto(w, c0):
                return lambda j: load_chunk(w, j, c0)

            W_IN, W_OUT, W_IN2, W_O = w_in[0], w_out[0], w_in_2[0], w_o_2[0]
            for s in range(ST):
                sp.dma_start(X[:, s, :], x[0, s * P:(s + 1) * P, :]).then_inc(x_landed, 16)
            for j in range(2):
                load_chunk(W_IN, j, 4 * N_A * HD, first=True)
            for t, r, src, n in [(0, C_NORM, norm_g, KT), (0, C_PREMIX, g_pre_mix_2, KT),
                                 (0, C_POSTMIX, g_post_mix_2, KT), (0, C_PREFFN, g_pre_ffn_2, KT),
                                 (0, C_POSTFFN, g_post_ffn_2, KT), (0, C_C, c_2, KT), (0, C_QLAT, g_q_lat_2, QT),
                                 (0, C_KVLAT, g_kv_lat_2, VT), (0, C_QN, q_norm_g, 1), (0, C_KN, k_norm_g, 1),
                                 (1, 0, b_ada_2, 6 * KT), (2, 0, conv_b_2, 2 * FT)]:
                sp.dma_start(PARAM[r:r + n, t, :], src.rearrange("a (r n) -> (a r) n", n=P)).then_inc(par_landed, 16)
            sp.dma_start(PARAM[0:2 * FT, 3:6, :], conv_w_2[0].rearrange("t (r n) -> r t n", n=P)).then_inc(par_landed, 16)
            C_B0 = 4 * N_A * HD
            for j in range(2, RING):
                load_chunk(W_IN, j, C_B0, first=True)
            sp.dma_start(sink[:], bass.AP(sinks_2.tensor, 0, [[0, P], [1, SWA_H]])).then_inc(misc_landed, 16)
            sp.dma_start(hot, bucket_hot).then_inc(misc_landed, 16)
            sp.wait_ge(const_ready, 1)
            sp.dma_start(table[0:BUCKETS, :], rel_bias_2).then_inc(misc_landed, 16)

            def g1_ada(kt0):
                def beside(i, slot):
                    if slot % 2 == 0:
                        load_ada(i * P + kt0 * P, (SH1, SC1)[slot // 4] * D + 1024 * (slot // 2 % 2))
                return beside

            def chunk_bias(h):
                b = n_bias[0] % 2
                n_bias[0] += 1
                sp.wait_ge(bias_used, T.free(bias_used))
                for q0 in (0, CHUNK):
                    first, end = 2 * P * b + CHUNK - q0, 2 * P * (b + 1)
                    src = bass.AP(rel_bias.tensor, h * N_REL, [[1, CHUNK], [1, end - first]])
                    sp.dma_start(bias[q0:q0 + CHUNK, first:end], src).then_inc(bias_landed[b], 16)

            def ada_and_bias(i, slot):
                if slot < 2:
                    chunk_bias(i * 2 + slot)
                g1_ada(6)(i, slot)

            panels(6, W_IN, C_B0, upto(W_IN, 0), g1_ada(0), free_ada_done=4)
            panels(4, W_IN, 0, upto(W_IN, 2048), ada_and_bias, free_ada_done=4, free_bias_used=2)
            panels(2, W_IN, 2048, upto(W_IN, 7168), g1_ada(10), free_ada_done=4)
            panels(2, W_IN, 7168, upto(W_IN, 3072), g1_ada(12), free_ada_done=4)
            panels(2, W_IN, 3072, upto(W_OUT, 0), g1_ada(14), free_ada_done=4)

            def ada_piece(part, kt0):
                def beside(i, slot):
                    if slot % 2 == 0:
                        load_ada(i * (2 * P) + (kt0 + slot // 4) * P, part * D + 1024 * (slot // 2 % 2))
                return beside

            panels(4, W_OUT, 0, upto(W_IN2, 0), ada_piece(SC2, 0), free_ada_done=4)
            C_KVS = LAT + SWA_H * SWA_D
            panels(3, W_IN2, 0, upto(W_IN2, C_KVS), ada_piece(SC2, 8), free_ada_done=4)
            uq = [(c0, k) for c0 in range(0, MLA_H * (HD + ROPE), 1024) for k in range(QT)]

            def load_uq(j):
                c0, k = uq[j]
                load(w_uq_2[0, P * k:P * (k + 1), c0:c0 + 1024])

            panels(1, W_IN2, C_KVS, load_uq, lambda i, slot: ada_piece(SC2, 14)(i, slot))
            for j in range(len(uq)):
                if j + RING < len(uq):
                    load_uq(j + RING)
                if j < KT:
                    load_ada(j // 2 * P, SH2 * D + 1024 * (j % 2))
                if j + RING >= len(uq):
                    r = j + RING - len(uq)
                    load_chunk(w_ukv_2[0], r % 2, PANEL * (r // 2))
            with T.loop(3, ready_lo_ready=4) as i:
                for j in range(4):
                    load_chunk(w_ukv_2[0], j % 2, i * 1024 + (1024 + PANEL * (j // 2)))
            for j in range(RING):
                load_chunk(W_IN2, j, LAT)
            C_G = C_KVS + 2 * SWA_G * SWA_D
            panels(4, W_IN2, LAT, upto(W_IN2, C_G))

            def window_bias(i, slot):
                ada_piece(GT1, 0)(i, slot)
                if slot >= 4:
                    return
                b = n_bias[0] % 2
                n_bias[0] += 1
                sp.wait_ge(bias_used, T.free(bias_used))
                src = bass.AP(win_dram.tensor, i * (8 * TOEP) + 2 * slot * TOEP, [[1, P], [TOEP, 2], [1, BAND]])
                sp.dma_start(bias[:, 2 * BAND * b:2 * BAND * (b + 1)].rearrange("p (e n) -> p e n", e=2), src)\
                  .then_inc(bias_landed[b], 16)

            sp.wait_ge(win_stored, 16)
            sp.wait_ge(s_read, T.ready(s_read, N_B + MLA_H))
            panels(4, W_IN2, C_G, upto(W_IN2, C_G + D), window_bias, free_bias_used=4,
                   free_ada_done=4)
            panels(4, W_IN2, C_G + D, upto(W_O, 0), ada_piece(GT1, 8), free_ada_done=4)

            def load_up(j, c0):
                src = w_up_2[0, 4 * P * (j // 2):4 * P * (j // 2 + 1), ds(c0 + (j % 2) * FF, 2 * P)]
                load(src.rearrange("(k p) n -> p k n", p=P))

            def load_down(kt, half):
                load(w_down_2[0, ds(kt * P, P), 1024 * half:1024 * (half + 1)])

            panels(4, W_O, 0, lambda j: load_up(j, 0), ada_piece(SH2, 8), free_ada_done=4)

            def up_panel(p, kt=None, last=False):
                for slot in range(SLOTS):
                    if slot + RING < SLOTS:
                        load_up(slot + RING, p * 256)
                    elif last:
                        load_down(slot // 2 - 2, slot % 2)
                    else:
                        load_up(slot + RING - SLOTS, p * 256 + 256)
                    if kt is not None and slot in (1, 5):
                        load_ada(kt * P, GT2 * D + 1024 * (slot // 4))

            up_panel(0)
            with T.loop(KT, ready_lo_ready=8, free_ada_done=2) as i:
                up_panel(i + 1, i)
            with T.loop(4, ready_lo_ready=8) as i:
                up_panel(i + (KT + 1))
            up_panel(21, last=True)
            with T.loop(FT // 2 - 1, ready_lo_ready=4) as i:
                for j in range(2):
                    for half in range(2):
                        load_down(i * 2 + (2 + j), half)
            for j in range(2 * ST):
                s, cols = j // 2, slice(1024 * (j % 2), 1024 * (j % 2 + 1))
                if j < 2 * ST - 1:
                    sp.wait_ge(fin_ready, j + 1)
                else:
                    sp.wait_ge(last_ready, 1)
                sp.dma_start(out[0, s * P:(s + 1) * P, cols], X[:, s, cols]).then_inc(stored, 16)
            sp.wait_ge(stored, 16 * 2 * ST)

        @block.gpsimd
        def _(pool):
            T = Tally(pool, credits)

            def select(dst, keep_if, base, channel, step, fill):
                return nc.gpsimd.affine_select(out=dst, in_=dst, compare_op=keep_if, fill=fill, base=base,
                                               pattern=[[step, dst.shape[1]]], channel_multiplier=channel)

            for k, (dst, v) in enumerate(((ident, 0.0), (ident_b, 0.0), (tri, -1.0), (below, 1.0), (neg_b, NEG),
                                          (ones, 1.0), (minus1, -1.0), (zero_c, 0.0))):
                nc.gpsimd.memset(dst[:], v).then_inc(pool_step, 1)
            nc.gpsimd.memset(bias[:], NEG).then_inc(pool_step, 1)
            nc.gpsimd.memset(table, NEG).then_inc(pool_step, 1)
            pool.wait_ge(pool_step, 10)
            select(ident[:], ALU.not_equal, 0, 1, -1, 1.0).then_inc(pool_step, 1)
            select(ident_b[:], ALU.not_equal, 0, 1, -1, 1.0).then_inc(pool_step, 1)
            select(tri[:], ALU.is_ge, 0, 1, -1, 0.0).then_inc(pool_step, 1)
            select(below[:], ALU.is_gt, 0, -1, 1, 0.0).then_inc(pool_step, 1)
            select(neg_b[:], ALU.is_ge, 0, 1, -1, 0.0).then_inc(pool_step, 1)
            pool.wait_ge(pool_step, 15)
            nc.gpsimd.nop().then_inc(const_ready, 1)
            nc.gpsimd.memset(ADA_1, 0.0).then_inc(acc_zeroed, 1)
            pool.wait_ge(par_T, 1)
            nc.gpsimd.memset(ADA_SC2, 0.0).then_inc(acc_zeroed, 1)
            pool.wait_ge(win_ready, 1)
            nc.gpsimd.dma_start(win_dram[:, 0:383], expanded).then_inc(win_stored, 16)

            def stage_sb(h):
                pool.wait_ge(sb_transposed, T.free(sb_transposed))
                nc.gpsimd.tensor_copy(stage[:, :, 0, :], QKV_A[:, :, ds(h * HD, HD)])
                nc.gpsimd.tensor_copy(stage[:, :, 1, :], QKV_A[:, :, ds(h * HD + N_A * HD, HD)])\
                    .then_inc(sb_staged, 1)

            pool.wait_ge(acc_free[1], credits["acc_free1"] + 9)
            pool.wait_ge(qk_transposed, credits["qk_transposed"] + N_B)
            with T.loop(2, free_sb_transposed=4) as i:
                for j in range(4):
                    stage_sb(i * 4 + j)

            pool.wait_ge(rows_T, 8 + 8)
            for s in range(ST):
                nc.gpsimd.dma_start(X[:, s, :], x[0, s * P:(s + 1) * P, :]).then_inc(x_again, 16)
            pool.wait_ge(s_read, credits["s_read"] + N_B)
            nc.gpsimd.memset(bias[:, 0:384], 0.0).then_inc(pool_step, 1)
            pool.wait_ge(pool_step, 16)
            select(bias[:, 0:P], ALU.is_ge, 0, 1, -1, NEG).then_inc(mask_ready, 1)
            select(bias[:, 2 * P:3 * P], ALU.is_ge, 0, 1, -1, NEG).then_inc(mask_ready, 1)

            def rope(dst, src, done):
                half = ROPE // 2
                nc.gpsimd.tensor_tensor(tmp_r[:, :, 0:half], src[:, :, half:ROPE], sinT[:, :, 0:half], ALU.mult)
                nc.gpsimd.tensor_tensor(tmp_r[:, :, half:ROPE], src[:, :, 0:half], sinT[:, :, half:ROPE], ALU.mult)
                nc.gpsimd.tensor_tensor(dst, src, cosT, ALU.mult).then_inc(pool_step, 1)
                pool.wait_ge(pool_step, T.ready(pool_step))
                nc.gpsimd.tensor_tensor(dst, dst, tmp_r, ALU.add).then_inc(done, 1)

            T.skip(pool_step, 16)
            pool.wait_ge(mod_ready, 1)
            nc.gpsimd.memset(ADA_SH2[0], 0.0).then_inc(acc_zeroed, 1)
            nc.gpsimd.dma_start(cosT, rope_cos.rearrange("(s p) n -> p s n", p=P)).then_inc(rope_landed, 16)
            nc.gpsimd.dma_start(sinT, rope_sin.rearrange("(s p) n -> p s n", p=P)).then_inc(rope_landed, 16)
            pool.wait_ge(rows_ready, 6)
            for s in range(ST):
                nc.gpsimd.dma_start(x1_dram[s * P:(s + 1) * P, :], X[:, s, :]).then_inc(x_saved, 16)
            pool.wait_ge(rope_landed, 32)
            pool.wait_ge(acc_free[1], credits["acc_free1"] + 16 + 4 + 3)
            rope(stage_r, KR[:], kr_staged)
            pool.wait_ge(kr_T, 1)

            def stage_mla(h):
                pool.wait_ge(qk_transposed, T.free(qk_transposed))
                nc.gpsimd.tensor_copy(stage[:, :, 0, :], Q[:, :, ds(h * (HD + ROPE), HD)])
                nc.gpsimd.tensor_copy(stage[:, :, 1, :], KV[:, :, ds(h * (2 * HD), HD)])
                rope(stage_r, Q[:, :, ds(h * (HD + ROPE) + HD, ROPE)], stage_full)

            pool.wait_ge(acc_free[1], credits["acc_free1"] + 16 + 4 + 4 + 6 + 1)
            T.skip(qk_transposed, N_B, "free")
            with T.loop(4, free_qk_transposed=4, ready_pool_step=4) as i:
                for j in range(4):
                    stage_mla(i * 4 + j)

            pool.wait_ge(o_ready, credits["o_ready"] + N_B + MLA_H // 2)
            nc.gpsimd.memset(ADA_GT1, 0.0).then_inc(acc_zeroed, 1)

            def stage_swa(group, j):
                pool.wait_ge(qk_transposed, T.free(qk_transposed))
                last = nc.gpsimd.tensor_copy(stage[:, :, 0, :], QS[:, :, ds(group * PANEL + j * P, P)])
                if j == 0:
                    for e in range(2):
                        last = nc.gpsimd.tensor_copy(stage[:, :, 1, e * SWA_D:(e + 1) * SWA_D],
                                                     KVS[:, :, ds(group * SWA_D, SWA_D)])
                last.then_inc(stage_full, 1)

            pool.wait_ge(acc_free[1], credits["acc_free1"] + 16 + 4 + 4 + 6 + 8 + 1)
            with T.loop(4, free_qk_transposed=4) as i:
                for j in range(4):
                    stage_swa(i, j)
            pool.wait_ge(o_ready, credits["o_ready"] + N_B + MLA_H)
            nc.gpsimd.memset(ADA_SH2[1], 0.0).then_inc(acc_zeroed, 1)
            nc.gpsimd.dma_start(G_MIX, bass.AP(g_post_mix_2.tensor, 0, [[0, P], [1, D]])).then_inc(row_landed, 16)
            pool.wait_ge(x_saved, 32)
            pool.wait_ge(gates_used, credits["gates_used"] + 4 + 4 + 4)
            nc.gpsimd.dma_start(B_MIX, bass.AP(b_ada_2.tensor, GT1 * D, [[0, P], [1, D]])).then_inc(row_landed, 16)
            for s in range(ST):
                nc.gpsimd.dma_start(X[:, s, :], x1_dram[s * P:(s + 1) * P, :]).then_inc(x_again, 16)
            pool.wait_ge(rows_T, 8 + 8 + 8 + 5 + 8)
            nc.gpsimd.memset(ADA_GT2, 0.0).then_inc(acc_zeroed, 1)
            pool.wait_ge(acc_zeroed, 6)
            nc.gpsimd.dma_start(ADA_GT2[0:1, :], b_ada_2[:, GT2 * D:(GT2 + 1) * D]).then_inc(ffn_row_landed, 16)
            pool.wait_ge(rows_ready, 12)
            nc.gpsimd.dma_start(G_FFN, bass.AP(g_post_ffn_2.tensor, 0, [[0, P], [1, D]])).then_inc(ffn_row_landed, 16)
            for j in range(2 * ST - 1):
                cols = slice(1024 * (j % 2), 1024 * (j % 2 + 1))
                pool.wait_ge(y_scaled, j + 1)
                nc.gpsimd.tensor_tensor(X[:, j // 2, cols], X[:, j // 2, cols], H_FFN[:, j // 2, cols], ALU.add)\
                    .then_inc(fin_ready, 1)

        @block.scalar
        def _(act):
            T = Tally(act, credits)
            n = [0]

            def split():
                m = n[0]
                n[0] += 1
                act.wait_ge(landed[m % RING], T.ready(landed[m % RING], 16))
                act.wait_ge(chunk_used, T.free(chunk_used))
                nc.scalar.activation(w_hi[:, m % RING, :], raw[:, m % RING, :], ACT.Copy).then_inc(hi_ready, 1)

            give(act, "qkT_full", "pT_full", "sb_qkT", "sb_w_done")
            nc.scalar.preload_act_table_set("natural_log_exp_and_others")

            def square(src, total):
                width = src.shape[-1]
                dst = full[:, 0:width] if width <= PANEL else \
                    PS[:, B_T:B_T + 4, :].rearrange("p b n -> p (b n)")[:, 0:width]
                nc.scalar.activation(dst, src, ACT.Square, accum_out=total).then_inc(act_step, 1)
                act.wait_ge(act_step, T.ready(act_step))

            def root(at, n=ST):
                act.wait_ge(std_ready, T.ready(std_ready))
                r = stat[:, 8 + at:8 + at + n]
                nc.scalar.activation(r, stat[:, at:at + n], ACT.Ln).then_inc(act_step, 1)
                act.wait_ge(act_step, T.ready(act_step))
                nc.scalar.activation(r, r, ACT.Exp, scale=-0.5).then_inc(var_ready, 1)

            def columns_hi(j, dst, gain=None, shift=None, banks=B_T):
                act.wait_ge(rows_T, T.ready(rows_T))
                bank = PS[:, banks + j % 4, :]
                if gain is None:
                    last = nc.scalar.activation(dst[:, 2 * j:2 * j + 2, :].rearrange("p k t -> p (k t)"), bank,
                                                ACT.Copy)
                else:
                    for k in range(2):
                        last = nc.scalar.activation(dst[:, 2 * j + k, :], bank[:, SEQ * k:SEQ * (k + 1)],
                                                    ACT.Identity, bias=shift(2 * j + k), scale=gain(2 * j + k))
                last.then_inc(aT_hi_ready, 1)

            def first_panel(*columns, **banks):
                for slot in range(SLOTS):
                    for j in COLUMNS[slot]:
                        columns_hi(j, *columns, **banks)
                    split()

            def after_T(kind, j=0):
                act.wait_ge(qk_transposed, T.ready(qk_transposed))
                act.wait_ge(scores_done, T.free(scores_done))
                if kind == "b":
                    nc.scalar.activation(qkT[:, 0:SEQ], PS[:, B_T, 0:SEQ], ACT.Copy, scale=col[:, C_QN:C_QN + 1])
                    last = nc.scalar.activation(qkT[:, SEQ:], PS[:, B_T, SEQ:], ACT.Copy, scale=col[:, C_KN:C_KN + 1])
                else:
                    if kind == "mla":
                        nc.scalar.activation(qrT, PS[0:ROPE, B_S1, 0:SEQ], ACT.Copy)
                    w = SEQ if kind == "swa" and j else 2 * SEQ
                    last = nc.scalar.activation(qkT[:, 0:w], PS[:, B_T, 0:w], ACT.Copy)
                last.then_inc(qkT_full, 1)

            def after_S(kind, i=None, j=None):
                act.wait_ge(nm_full, T.ready(nm_full))
                act.wait_ge(p_transposed, T.free(p_transposed))
                n = 2 if kind == "swa" else 1

                def by_tile(at):
                    return smx[:, at:at + 4].rearrange("p (t e) -> p t e", t=ST)

                for e in range(n):
                    if kind == "swa":
                        nc.scalar.activation(by_tile(12)[:, :, e], by_tile(4)[:, :, e], ACT.Exp,
                                             bias=sink[:, ds(i * 8 + (2 * j + e), 1)])
                    for t, (a, b) in enumerate(((0, P), (P, 384))):
                        last = nc.scalar.activation(s_sb[:, e, a:b], s_sb[:, e, a:b], ACT.Exp,
                                                    bias=smx[:, 4 + n * t + e:5 + n * t + e],
                                                    accum_out=smx[:, 8 + n * t + e:9 + n * t + e])
                last.then_inc(p_done, 1)

            def after_P(kind):
                act.wait_ge(p_transposed, T.ready(p_transposed))
                act.wait_ge(o_ready, T.free(o_ready))
                for e in range(2 if kind == "swa" else 1):
                    last = nc.scalar.activation(pT[:, e, :], PS[:, B_P + e, 0:384], ACT.Copy)
                last.then_inc(pT_full, 1)

            def squares_b(p):
                for s in range(ST):
                    act.wait_ge(acc_free[s], T.ready(acc_free[s]))
                    for j in range(PANEL // HD):
                        nc.scalar.activation(full[:, 0:HD], QKV_B[:, s, ds(p * PANEL + j * HD, HD)], ACT.Square,
                                             accum_out=mean_b[:, s, ds(p * (PANEL // HD) + j, 1)]).then_inc(act_step, 1)
                        act.wait_ge(act_step, T.ready(act_step))

            def sb_T():
                act.wait_ge(sb_transposed, T.ready(sb_transposed))
                act.wait_ge(sb_zdone, T.free(sb_zdone))
                nc.scalar.activation(qkT[:, 0:SEQ], PS[:, B_T, 0:SEQ], ACT.Copy, scale=float(HD ** -0.5))
                nc.scalar.activation(qkT[:, SEQ:], PS[:, B_T, SEQ:], ACT.Copy).then_inc(sb_qkT, 1)

            def sb_Z(b):
                act.wait_ge(sb_zdone, T.ready(sb_zdone))
                act.wait_ge(sb_cum, T.free(sb_cum))
                for e, w in ((0, SEQ), (1, P)):
                    nc.scalar.activation(s_sb[:, e, 0:w], PS[:, B_Z[b][e], 0:w], ACT.Abs).then_inc(act_step, 1)
                act.wait_ge(act_step, T.ready(act_step, 2))
                for e, w in ((0, SEQ), (1, P)):
                    nc.scalar.activation(s_sb[:, e, 0:w], s_sb[:, e, 0:w], ACT.Exp, scale=-1.0).then_inc(act_step, 1)
                act.wait_ge(act_step, T.ready(act_step, 2))
                for e, w in ((0, SEQ), (1, P)):
                    last = nc.scalar.activation(s_sb[:, e, 0:w], s_sb[:, e, 0:w], ACT.Ln, bias=1.0)
                last.then_inc(sb_ln, 1)

            def sb_C(b):
                act.wait_ge(sb_cum, T.ready(sb_cum))
                act.wait_ge(sb_o_ready, T.free(sb_o_ready))
                nc.scalar.activation(pT[:, 0, 0:SEQ], PS[:, B_Z[b][0], 0:SEQ], ACT.Exp)
                nc.scalar.activation(pT[:, 1, 0:P], PS[:, B_Z[b][1], 0:P], ACT.Exp).then_inc(sb_w_done, 1)

            def products(s, chunks=SLOTS):
                if s == 0:
                    act.wait_ge(acc_ready, T.ready(acc_ready))
                else:
                    act.wait_ge(chunk_used, T.ready(chunk_used, chunks))

            def copy_out(dst, chunks=SLOTS):
                for s in range(ST):
                    products(s, chunks)
                    d = dst(s)
                    nc.scalar.activation(d, PS[:, s, 0:d.shape[-1]], ACT.Copy).then_inc(acc_free[s], 1)

            def gate(func, gates=GATES[1]):
                nc.scalar.activation(spare[:], zero_c[:], func).then_inc(act_step, 1)
                act.wait_ge(act_step, T.ready(act_step))
                act.wait_ge(gates_used, T.free(gates_used))
                for s in range(ST):
                    products(s)
                    nc.scalar.activation(gates[:, s, :], PS[:, s, :], func).then_inc(acc_free[s], 1)

            SP_ = ACT_PANEL
            act.wait_ge(x_landed, 16 * ST)
            for s in range(ST):
                square(X[:, s, :], squares[:, s:s + 1])
            act.nop().then_inc(var_ready, 1)
            root(0)
            act.wait_ge(par_ready, 1)
            nc.scalar.activation(silu_c[:], col[:, C_C:C_C + KT], ACT.Exp, scale=-1.0).then_inc(silu_ready, 1)
            for _ in range(AHEAD):
                split()
            act.wait_ge(const_ready, 1)
            first_panel(aT_hi, lambda k: col[:, C_NORM + k:C_NORM + k + 1], lambda k: zero_c[:])
            squares_b(0)
            with T.loop(3, **SP_, ready_act_step=2 * PANEL // HD, ready_acc_free0=1, ready_acc_free1=1) as i:
                for slot in range(SLOTS):
                    split()
                squares_b(i + 1)
            act.nop().then_inc(sums_b_ready, 1)
            for slot in range(SLOTS):
                split()
            act.wait_ge(mean_b_ready, 1)
            nc.scalar.activation(inv_b[:], mean_b[:], ACT.Ln).then_inc(act_step, 1)
            act.wait_ge(act_step, T.ready(act_step))
            nc.scalar.activation(inv_b[:], inv_b[:], ACT.Exp, scale=-0.5).then_inc(inv_b_ready, 1)
            for slot in range(SLOTS):
                split()
            T.skip(acc_ready, 6)
            T.skip(chunk_used, 6 * SLOTS)
            act.wait_ge(win_stored, 16)
            GATED = dict(**SP_, ready_acc_ready=1, ready_chunk_used=8)
            with T.loop(4, **GATED, ready_qk_transposed=2, free_scores_done=2,
                        ready_nm_full=2, ready_p_transposed=2, free_p_transposed=2, free_o_ready=2) as i:
                for slot in range(SLOTS):
                    split()
                    if slot - 3 in START_B:
                        after_P("b")
                    if slot - 2 in START_B:
                        after_S("b")
                    if slot in START_B:
                        after_T("b")
                copy_out(lambda s: QKV_A[:, s, ds(i * PANEL, PANEL)])
            T.skip(acc_ready, 2)
            T.skip(chunk_used, 2 * SLOTS)
            with T.loop(2, **SP_) as i:
                for slot in range(SLOTS):
                    split()

            def heads(slot, start, before):
                if h := due(slot, 3, start, before):
                    sb_C(h[2] % 2) if h[0] == "sb" else after_P(h[0])
                if (h := due(slot, 2, start, before)) and h[0] != "sb":
                    after_S(*h)
                if (h := due(slot, 1, start, before)) and h[0] == "sb":
                    sb_Z(h[2] % 2)
                if h := due(slot, 0, start, before):
                    sb_T() if h[0] == "sb" else after_T(h[0], h[2])

            def panel(start=None, before=None, func=None, gates=GATES[1]):
                for slot in range(SLOTS):
                    split()
                    if slot == SLOTS - 1 and func is not None:
                        gate(func, gates)
                        if func == ACT.Silu:
                            nc.scalar.preload_act_table_set("natural_log_exp_and_others")
                    heads(slot, start, before)

            for start, before in ((("sb", 0), None), (("sb", 1), ("sb", 0)), (None, ("sb", 1)), (None, None)):
                panel(start, before, ACT.Silu, GATES[0])
            for s in range(ST):
                T.skip(acc_free[s], 12)

            def x1_squares(p):
                for s in range(ST):
                    act.wait_ge(acc_free[s], T.ready(acc_free[s]))
                    square(X[:, s, ds(p * PANEL, PANEL)], squares[:, ds(p + 4 * s, 1)])

            first_panel(aT_hi)
            nc.scalar.preload_act_table_set("natural_log_exp_and_others")
            x1_squares(0)
            with T.loop(3, **SP_, ready_act_step=2, ready_acc_free0=1, ready_acc_free1=1) as i:
                for slot in range(SLOTS):
                    split()
                x1_squares(i + 1)
            act.nop().then_inc(var_ready, 1)
            T.skip(acc_ready, 4)
            T.skip(chunk_used, 4 * SLOTS)
            root(0)
            act.wait_ge(mod_ready, T.ready(mod_ready, 2))
            first_panel(aT_hi, lambda k: gains[:, 0, k:k + 1], lambda k: mod[:, SH1, k:k + 1])
            copy_out(lambda s: LATR[:, s, 0:PANEL])
            for slot in range(SLOTS):
                split()
            copy_out(lambda s: LATR[:, s, PANEL:2 * PANEL])
            for slot in range(SLOTS):
                split()
            for s in range(ST):
                products(s)
                nc.scalar.activation(KR[:, s, :], PS[:, s, LAT - 2 * PANEL - ROPE:LAT - 2 * PANEL], ACT.Copy)
                nc.scalar.activation(LATR[:, s, 2 * PANEL:LAT], PS[:, s, 0:LAT - 2 * PANEL], ACT.Copy)\
                    .then_inc(acc_free[s], 1)
            for slot in range(SLOTS):
                split()
                if slot == 0:
                    for s in range(ST):
                        act.wait_ge(acc_free[s], 1 + 16 + 4 + 3)
                        square(LATR[:, s, 0:Q_RANK], squares[:, s:s + 1])
                        square(LATR[:, s, Q_RANK:Q_RANK + KV_RANK], squares[:, ST + s:ST + s + 1])
                    act.nop().then_inc(var_ready, 1)
                if slot == 1:
                    root(2, 2 * ST)
                if slot >= 3:
                    columns_hi(slot - 3, latT_hi, lambda k: col[:, C_QLAT + k:C_QLAT + k + 1], lambda k: zero_c[:])
            copy_out(lambda s: KVS[:, s, :])
            act.wait_ge(kr_T, 1)
            nc.scalar.activation(krT, PS[0:ROPE, B_O, 0:SEQ], ACT.Copy).then_inc(kr_ready, 1)
            act.wait_ge(x_saved, 32)
            for c in range(3):
                for _ in range(QT):
                    split()
                for half in range(2):
                    for s in range(ST):
                        products(s if half else 0, QT)
                        nc.scalar.activation(Q[:, s, 1024 * c + PANEL * half:1024 * c + PANEL * (half + 1)],
                                             PS[:, 2 * half + s, :], ACT.Copy).then_inc(acc_free[s], 1)
            with T.loop(4, **LANDED, free_chunk_used=4, ready_acc_ready=2, ready_chunk_used=4) as i:
                for j in range(2):
                    split()
                    split()
                    copy_out(lambda s: KV[:, s, ds(i * 1024 + PANEL * j, PANEL)], VT // 2)
            nc.scalar.preload_act_table_set("natural_log_exp_and_others")
            HEADS4 = dict(ready_qk_transposed=4, free_scores_done=4, ready_nm_full=4, ready_p_transposed=4,
                          free_p_transposed=4, free_o_ready=4)
            panel(("mla", 0))
            with T.loop(3, **SP_, **HEADS4) as i:
                panel(("mla", i + 1), ("mla", i))
            T.skip(acc_ready, 4)
            T.skip(chunk_used, 4 * SLOTS)
            panel(("swa", 0), ("mla", 3), ACT.Sigmoid)
            with T.loop(3, **GATED, **HEADS4, ready_act_step=1, free_gates_used=1) as i:
                panel(("swa", i + 1), ("swa", i), ACT.Sigmoid)
            panel(None, ("swa", 3), ACT.Sigmoid)
            with T.loop(3, **GATED, ready_act_step=1, free_gates_used=1) as i:
                panel(func=ACT.Sigmoid)
            def mix_squares(p):
                for s in range(ST):
                    products(s)
                    square(PS[:, s, :], squares[:, ds(p + 4 * s, 1)])
                    act.nop().then_inc(gate_ready, 1)

            first_panel(aT_hi)
            nc.scalar.preload_act_table_set("natural_log_exp_and_others")
            mix_squares(0)
            with T.loop(3, **GATED, ready_act_step=2) as i:
                for slot in range(SLOTS):
                    split()
                mix_squares(i + 1)
            act.nop().then_inc(var_ready, 1)
            root(0)
            for j in range(2 * ST):
                s, half = j // 2, j % 2
                act.wait_ge(x2_ready, j + 1)
                square(X[:, s, 1024 * half:1024 * (half + 1)], squares[:, 2 * s + half:2 * s + half + 1])
            act.nop().then_inc(var_ready, 1)
            root(2)
            act.wait_ge(mod_ready, T.ready(mod_ready, 4))

            def taps(pair, b, bank):
                if b == 0:
                    act.wait_ge(chunk_used, T.ready(chunk_used, SLOTS))
                act.wait_ge(y_done, T.free(y_done))
                for k, (dst, tile) in enumerate(((conv_g[b], pair), (conv_u[b], pair + FT))):
                    last = nc.scalar.activation(dst, PS[:, bank + 2 * k, 0:SEQ], ACT.Identity,
                                                bias=col[:, ds(tile + C_CONVB, 1)],
                                                scale=col[:, ds(tile + (C_CONVW + 2 * P), 1)])
                last.then_inc(conv_a, 1)

            def silu(b):
                act.wait_ge(conv_d, T.ready(conv_d))
                nc.scalar.activation(conv_g[b], conv_g[b], ACT.Silu).then_inc(conv_s, 1)

            def up_panel(before, odd):
                for slot in range(SLOTS):
                    split()
                    if slot < 2:
                        taps(before + slot, slot, (0 if odd else B_UP1) + slot)
                    if slot in (3, 4):
                        silu(slot - 3)

            first_panel(aT_hi, lambda k: gains[:, 1, k:k + 1], lambda k: mod[:, SH2, k:k + 1], banks=B_UP1)
            with T.loop(10, **{k: 4 * v for k, v in LANDED.items()}, free_chunk_used=16,
                        ready_chunk_used=16, free_y_done=4, ready_conv_d=4) as i:
                up_panel(i * 4, True)
                up_panel(i * 4 + 2, False)
            up_panel(40, True)
            for b in range(2):
                taps(42 + b, b, B_UP1 + b)
            act.wait_ge(spread_done, 3)
            nc.scalar.activation(ADA_GT2, PS[:, 0:4, :].rearrange("p b n -> p (b n)"), ACT.Copy).then_inc(g_copied, 1)
            for b in range(2):
                silu(b)

            def y_split(kt, slot):
                nc.scalar.activation(aT_hi[:, slot, :], YT[:, ds(kt, 1), :].rearrange("p a t -> p (a t)"),
                                     ACT.Copy).then_inc(y_hi, 1)

            y_split(0, 0)
            act.wait_ge(y_done, credits["y_done"] + FT)
            with T.loop(FT // 2 - 1, **LANDED, free_chunk_used=4) as i:
                for j in range(2):
                    split()
                    y_split(i * 2 + (j + 1), (j + 1) % 2)
                    split()
            split()
            y_split(FT - 1, 1)
            nc.scalar.preload_act_table_set("natural_log_exp_and_others")
            for s in range(ST):
                act.wait_ge(down_done, s + 1)
                nc.scalar.activation(H_FFN[:, s, :], PS[:, 4 * s:4 * s + 4, :].rearrange("p b n -> p (b n)"),
                                     ACT.Square, accum_out=stat[:, s:s + 1]).then_inc(var_ready, 1)
                root(s, 1)

        @block.vector
        def _(dve):
            T = Tally(dve, credits)
            n = [0]

            def split():
                m = n[0]
                n[0] += 1
                dve.wait_ge(hi_ready, T.ready(hi_ready))
                nc.vector.tensor_tensor(w_lo[:, m % RING, :], raw[:, m % RING, :], w_hi[:, m % RING, :].bitcast(F32),
                                        ALU.subtract).then_inc(lo_ready, 1)

            def link(ins):
                ins.then_inc(dve_step, 1)
                dve.wait_ge(dve_step, T.ready(dve_step))

            give(dve, "acc_free0", "acc_free1", "ada_done", "s_read", "o_done", "bias_used", "conv_d", "y_done", "gates_used",
                 "sb_o_done")

            def products(s, chunks=SLOTS):
                if s == 0:
                    dve.wait_ge(acc_ready, T.ready(acc_ready))
                else:
                    dve.wait_ge(chunk_used, T.ready(chunk_used, chunks))

            def gated(s, squares=False):
                if squares:
                    dve.wait_ge(gate_ready, T.ready(gate_ready))
                else:
                    dve.wait_ge(acc_free[s], T.ready(acc_free[s]))
                if s == 0:
                    T.skip(acc_ready)
                else:
                    T.skip(chunk_used, SLOTS)

            def copy_out(dst, chunks=SLOTS):
                for s in range(ST):
                    products(s, chunks)
                    d = dst(s)
                    nc.vector.tensor_copy(d, PS[:, s, 0:d.shape[-1]]).then_inc(acc_free[s], 1)

            def gate_out(dst):
                for s in range(ST):
                    gated(s)
                    last = nc.vector.tensor_tensor(dst(s), dst(s), GATES[0][:, s, :], ALU.mult)
                last.then_inc(gates_used, 1)

            def ada(acc, half, kt):
                j = n_ada[0] % 2
                n_ada[0] += 1
                dve.wait_ge(ada_landed[j], T.ready(ada_landed[j], 16))
                part = acc[:, 1024 * half:1024 * (half + 1)]
                dve.wait_ge(ada_done, T.ready(ada_done, 0))
                nc.vector.scalar_tensor_tensor(out=part, in0=ada_raw[:, j, :], scalar=silu_c[:, ds(kt, 1)],
                                               in1=part, op0=ALU.mult, op1=ALU.add).then_inc(ada_done, 1)
                T.skip(ada_done)

            n_ada = [0]

            def mod_columns(parts, more=False):
                dve.wait_ge(ada_cols, T.ready(ada_cols))
                for j, part in enumerate(parts):
                    base = mod[:, part, :] if more else col[:, C_ADA + KT * part:C_ADA + KT * (part + 1)]
                    last = nc.vector.tensor_tensor(mod[:, part, :], PS[:, B_O, KT * j:KT * (j + 1)], base, ALU.add)
                last.then_inc(mod_ready, 1)
                T.skip(mod_ready)

            def gain(j, g, part):
                dve.wait_ge(mod_ready, T.ready(mod_ready, 0))
                nc.vector.scalar_tensor_tensor(out=gains[:, j, :], in0=mod[:, part, :], scalar=1.0,
                                               in1=col[:, g:g + KT], op0=ALU.add, op1=ALU.mult).then_inc(mod_ready, 1)
                dve.wait_ge(mod_ready, T.ready(mod_ready))

            def mean(at, widths, parts=1):
                dve.wait_ge(var_ready, T.ready(var_ready))
                n = ST * len(widths)
                v = stat[:, at:at + n]
                link(nc.vector.tensor_reduce(v, squares[:, 0:n * parts].rearrange("p (s j) -> p s j", s=n), AX.X,
                                             ALU.add))
                for j, width in enumerate(widths):
                    last = nc.vector.tensor_scalar(v[:, ST * j:ST * (j + 1)], v[:, ST * j:ST * (j + 1)], 1.0 / width,
                                                   EPS, ALU.mult, ALU.add)
                last.then_inc(std_ready, 1)

            def newton(r, v, t):
                link(nc.vector.tensor_tensor(t, r, r, ALU.mult))
                link(nc.vector.scalar_tensor_tensor(out=t, in0=t, scalar=-0.5, in1=v, op0=ALU.mult, op1=ALU.mult))
                link(nc.vector.scalar_tensor_tensor(out=r, in0=t, scalar=1.5, in1=r, op0=ALU.add, op1=ALU.mult))

            def inverse_rms(at, n=ST):
                dve.wait_ge(var_ready, T.ready(var_ready))
                newton(stat[:, 8 + at:8 + at + n], stat[:, at:at + n], smx[:, 0:n])

            def diagonals(at, n=ST):
                for j in range(n):
                    last = nc.vector.tensor_scalar(diag[:, j, :], ident[:], stat[:, 8 + at + j:9 + at + j], None,
                                                   ALU.mult)
                last.then_inc(rows_ready, 2)

            def columns_lo(j, dst, hi, gain=None, shift=None, banks=B_T):
                dve.wait_ge(aT_hi_ready, T.ready(aT_hi_ready))
                bank = PS[:, banks + j % 4, :]
                if gain is not None and shift is None:
                    for k in range(2):
                        last = nc.vector.scalar_tensor_tensor(
                            out=dst[:, 2 * j + k, :], in0=bank[:, SEQ * k:SEQ * (k + 1)], scalar=gain(2 * j + k),
                            in1=hi[:, 2 * j + k, :].bitcast(F32), op0=ALU.mult, op1=ALU.subtract)
                    last.then_inc(aT_ready, 1)
                    T.skip(aT_ready)
                    return
                if gain is not None:
                    dve.wait_ge(aT_ready, T.ready(aT_ready, 0))
                    for k in range(2):
                        last = nc.vector.tensor_scalar(full[:, SEQ * k:SEQ * (k + 1)], bank[:, SEQ * k:SEQ * (k + 1)],
                                                       gain(2 * j + k), shift(2 * j + k), ALU.mult, ALU.add)
                    link(last)
                    bank = full
                nc.vector.tensor_tensor(dst[:, 2 * j:2 * j + 2, :].rearrange("p k t -> p (k t)"), bank,
                                        hi[:, 2 * j:2 * j + 2, :].rearrange("p k t -> p (k t)").bitcast(F32),
                                        ALU.subtract).then_inc(aT_ready, 1)
                T.skip(aT_ready)

            def descending(at, n, heads=1):
                whole = bias[:, :]
                return bass.AP(whole.tensor, whole.offset + at + n - 1,
                               [list(whole.ap[0])] + ([[BAND, heads]] if heads > 1 else []) + [[-1, n]])

            def first_panel(beside, *columns, **banks):
                for slot in range(SLOTS):
                    for j in COLUMNS[slot]:
                        columns_lo(j, *columns, **banks)
                    split()
                    beside(slot)

            def softmax(kind, scale, i=None, j=None):
                b = None if j is None else j % 2
                dve.wait_ge(scores_done, T.ready(scores_done))
                dve.wait_ge(p_transposed, T.free(p_transposed))
                if kind == "b":
                    dve.wait_ge(bias_landed[b], T.ready(bias_landed[b], 32))
                elif kind == "swa":
                    dve.wait_ge(bias_landed[b], T.ready(bias_landed[b], 16))
                n = 2 if kind == "swa" else 1
                for t, (lo, hi) in enumerate(((0, P), (P, 384))):
                    if kind == "mla":
                        mask = bias[:, lo:hi]
                    elif kind == "b":
                        mask = descending(2 * P * b, hi - lo)
                    else:
                        mask = descending(2 * BAND * b, hi - lo, 2)
                    last = nc.vector.scalar_tensor_tensor(
                        out=s_sb[:, 0:n, lo:hi] if n == 2 else s_sb[:, 0, lo:hi],
                        in0=PS[:, B_S0:B_S0 + n, lo:hi] if n == 2 else PS[:, B_S0, lo:hi],
                        scalar=scale, in1=mask, op0=ALU.mult, op1=ALU.add)
                last.then_inc(s_read, 1)
                dve.wait_ge(s_read, T.ready(s_read))
                top = smx[:, 0:2 * n].rearrange("p (t e) -> p t e", t=ST)
                for t, (lo, hi) in enumerate(((0, P), (P, 384))):
                    last = nc.vector.tensor_reduce(top[:, t, :], s_sb[:, 0:n, lo:hi], AX.X, ALU.max)
                if kind != "mla":
                    last.then_inc(bias_used, 1)
                    dve.wait_ge(bias_used, T.ready(bias_used))
                else:
                    link(last)
                if kind == "swa":
                    nc.vector.scalar_tensor_tensor(
                        out=smx[:, 4:8].rearrange("p (t e) -> p t e", t=ST), in0=top, scalar=-1.0,
                        in1=minus_sink[:, :, ds(i * 8 + 2 * j, 2)], op0=ALU.mult, op1=ALU.min).then_inc(nm_full, 1)
                else:
                    nc.vector.tensor_scalar(smx[:, 4:6], smx[:, 0:2], -1.0, None, ALU.mult).then_inc(nm_full, 1)

            def weigh(kind, b):
                wide = 4 if kind == "swa" else 2
                dve.wait_ge(p_done, T.ready(p_done))
                if kind == "swa":
                    link(nc.vector.tensor_tensor(smx[:, 16:20], smx[:, 8:12], smx[:, 12:16], ALU.add))
                    link(nc.vector.reciprocal(smx[:, 20 + 4 * b:24 + 4 * b], smx[:, 16:20]))
                else:
                    link(nc.vector.reciprocal(smx[:, 20 + 4 * b:20 + 4 * b + wide], smx[:, 8:8 + wide]))

            def heads_out(kind, b, dst):
                dve.wait_ge(o_ready, T.ready(o_ready))
                n = 2 if kind == "swa" else 1
                for e in range(n):
                    w = SWA_D if kind == "swa" else HD
                    for t in range(ST):
                        last = nc.vector.tensor_scalar(dst(t, e), PS[:, B_O, HD * t + w * e:HD * t + w * (e + 1)],
                                                       smx[:, 20 + 4 * b + n * t + e:21 + 4 * b + n * t + e],
                                                       None, ALU.mult)
                last.then_inc(o_done, 1)

            def stage_b(h):
                dve.wait_ge(qk_transposed, T.free(qk_transposed))
                src = QKV_B[:, :, 0:2 * N_B * HD].rearrange("p s (k n) -> p s k n", k=2)[:, :, :, ds(h * HD, HD)]
                r = inv_b[:, :, :].rearrange("p s (k h) -> p s k h", k=2)[:, :, :, ds(h, 1)].to_broadcast([P, ST, 2, HD])
                nc.vector.tensor_tensor(stage[:], src, r, ALU.mult).then_inc(stage_full, 1)

            def sb_P(b):
                dve.wait_ge(sb_ln, T.ready(sb_ln))
                for e, w in ((0, SEQ), (1, P)):
                    last = nc.vector.scalar_tensor_tensor(out=s_sb[:, e, 0:w], in0=PS[:, B_Z[b][e], 0:w], scalar=0.0,
                                                          in1=s_sb[:, e, 0:w], op0=ALU.max, op1=ALU.add)
                link(last)
                for e in range(2):
                    last = nc.vector.tensor_tensor(s_sb[:, e, 0:P], s_sb[:, e, 0:P], below[:], ALU.mult)
                last.then_inc(sb_spdone, 1)

            def sb_out(h):
                dve.wait_ge(sb_o_ready, T.ready(sb_o_ready))
                nc.vector.tensor_copy(QKV_A[:, :, ds(h * HD, HD)],
                                      PS[:, B_O, 0:2 * HD].rearrange("p (t n) -> p t n", t=ST)).then_inc(sb_o_done, 1)

            ADA = dict(ready_ada_landed0=32, ready_ada_landed1=32, ready_ada_done=4)
            DP = dict(**DVE_PANEL, ready_acc_ready=1, ready_chunk_used=8)
            G1 = dict(**DP, ready_ada_landed0=32, ready_ada_landed1=32, ready_ada_done=4)

            mean(0, [D])
            inverse_rms(0)
            dve.wait_ge(const_ready, 1)
            diagonals(0)
            dve.wait_ge(par_T, 1)
            for t, r in enumerate(PARAM_ROWS):
                last = nc.vector.tensor_copy(col[:, P * t:P * t + r], PS[:, 6 + t // 4, P * (t % 4):P * (t % 4) + r])
            last.then_inc(par_ready, 1)
            for _ in range(AHEAD):
                split()
            dve.wait_ge(silu_ready, 1)
            link(nc.vector.tensor_scalar(silu_c[:], silu_c[:], 1.0, None, ALU.add))
            link(nc.vector.reciprocal(silu_c[:], silu_c[:]))
            link(nc.vector.tensor_tensor(silu_c[:], silu_c[:], col[:, C_C:C_C + KT], ALU.mult))
            dve.wait_ge(acc_zeroed, 2)

            def g1(slot, kt):
                if slot % 2 == 0:
                    ada(ADA_1, slot // 2, kt)

            def g1_slot(slot, kt):
                split()
                g1(slot, kt)

            def ada_piece(acc, p, slot, kt0):
                if slot % 2 == 0:
                    ada(acc, slot // 2 % 2, p * 2 + (kt0 + slot // 4))

            def qkv_b(p):
                for slot in range(SLOTS):
                    g1_slot(slot, p)
                copy_out(lambda s: QKV_B[:, s, ds(p * PANEL, PANEL)])

            first_panel(lambda slot: g1(slot, 0), aT_lo, aT_hi, lambda k: col[:, C_NORM + k:C_NORM + k + 1])
            copy_out(lambda s: QKV_B[:, s, 0:PANEL])
            dve.wait_ge(win_cols, 1)
            nc.vector.tensor_copy(expanded, PS[0:SWA_H, B_O - 1, 0:383]).then_inc(win_ready, 1)
            with T.loop(4, **G1) as i:
                qkv_b(i + 1)
            dve.wait_ge(sums_b_ready, 1)
            v = mean_b[:]
            nc.vector.tensor_scalar(v, v, 1.0 / HD, EPS, ALU.mult, ALU.add).then_inc(mean_b_ready, 1)
            dve.wait_ge(inv_b_ready, 1)
            newton(inv_b[:], v, tmp_b[:])
            qkv_b(5)
            with T.loop(4, **DVE_PANEL, **ADA, free_qk_transposed=2, ready_dve_step=2, ready_scores_done=2,
                        free_p_transposed=2, ready_bias_landed0=32, ready_bias_landed1=32, ready_s_read=2,
                        ready_bias_used=2, ready_p_done=2, ready_o_ready=2) as i:
                for slot in range(SLOTS):
                    g1_slot(slot, i + 6)
                    if slot - 4 in START_B:
                        b = START_B.index(slot - 4)
                        heads_out("b", b, lambda t, e: QKV_B[:, t, ds(i * (2 * HD) + b * HD, HD)])
                    if slot - 3 in START_B:
                        weigh("b", START_B.index(slot - 3))
                    if slot - 1 in START_B:
                        softmax("b", float(HD ** -0.5), j=START_B.index(slot - 1))
                    if slot + 1 in START_B:
                        stage_b(i * 2 + START_B.index(slot + 1))
            T.skip(acc_ready, 4)
            T.skip(chunk_used, 4 * SLOTS)
            with T.loop(2, **G1) as i:
                for slot in range(SLOTS):
                    g1_slot(slot, i + 10)
                copy_out(lambda s: QKV_A[:, s, ds(i * PANEL + 2048, PANEL)])

            def out_of(kind, i, j):
                if kind == "mla":
                    return lambda t, e: Q[:, t, ds(i * (4 * (HD + ROPE)) + j * (HD + ROPE), HD)]
                return lambda t, e: QS[:, t, ds(i * PANEL + (P * j + SWA_D * e), SWA_D)]

            def heads(slot, start, before):
                if h := due(slot, 4, start, before):
                    sb_out(h[1] * 4 + h[2]) if h[0] == "sb" else heads_out(h[0], h[2] % 2, out_of(*h))
                if (h := due(slot, 3, start, before)) and h[0] != "sb":
                    weigh(h[0], h[2] % 2)
                if (h := due(slot, 2, start, before)) and h[0] == "sb":
                    sb_P(h[2] % 2)
                if (h := due(slot, 1, start, before)) and h[0] != "sb":
                    softmax(h[0], float((HD + ROPE) ** -0.5 if h[0] == "mla" else SWA_D ** -0.5), h[1], h[2])

            for s in range(ST):
                T.skip(acc_free[s], 12)
            for p, (start, before) in enumerate(((("sb", 0), None), (("sb", 1), ("sb", 0)), (None, ("sb", 1)),
                                                 (None, None))):
                for slot in range(SLOTS):
                    g1_slot(slot, p + 12)
                    heads(slot, start, before)
                gate_out(lambda s: (QKV_B if p < 2 else QKV_A)[:, s, ds(p % 2 * PANEL, PANEL)])
            dve.wait_ge(gates_used, credits["gates_used"] + 4)
            nc.vector.nop().then_inc(rows_ready, 2)
            OUTP = dict(**DP, **ADA)

            def add_out(c0):
                dve.wait_ge(x_again, 32)
                for s in range(ST):
                    products(s)
                    nc.vector.tensor_tensor(X[:, s, ds(c0, PANEL)], X[:, s, ds(c0, PANEL)], PS[:, s, :],
                                            ALU.add).then_inc(acc_free[s], 1)

            first_panel(lambda slot: ada_piece(ADA_SC2, 0, slot, 0), aT_lo, aT_hi)
            add_out(0)
            with T.loop(3, **OUTP) as i:
                for slot in range(SLOTS):
                    split()
                    ada_piece(ADA_SC2, i + 1, slot, 0)
                add_out((i + 1) * PANEL)
            mod_columns((SH1, SC1))
            gain(0, C_PREMIX, SC1)
            mean(0, [D], 4)
            inverse_rms(0)
            diagonals(0)
            first_panel(lambda slot: ada_piece(ADA_SC2, 0, slot, 8), aT_lo, aT_hi, lambda k: gains[:, 0, k:k + 1],
                        lambda k: mod[:, SH1, k:k + 1])
            for p in (1, 2):
                for slot in range(SLOTS):
                    split()
                    ada_piece(ADA_SC2, p, slot, 8)
            for slot in range(SLOTS):
                split()
                ada_piece(ADA_SC2, 3, slot, 8)
                if slot == 0:
                    mean(2, [Q_RANK, KV_RANK])
                if slot == 1:
                    inverse_rms(2, 2 * ST)
                    diagonals(2, 2 * ST)
                if slot >= 3:
                    columns_lo(slot - 3, latT_lo, latT_hi, lambda k: col[:, C_QLAT + k:C_QLAT + k + 1])
            T.skip(acc_ready, 4)
            T.skip(chunk_used, 4 * SLOTS)
            dve.wait_ge(acc_zeroed, 3)
            for c in range(3):
                for k in range(QT):
                    split()
                    if c * QT + k < KT:
                        ada(ADA_SH2[0], (c * QT + k) % 2, (c * QT + k) // 2)
                if c == 1:
                    mod_columns((SC2,))
                    gain(1, C_PREFFN, SC2)
            T.skip(acc_ready, 3 * 3 + 8)
            T.skip(chunk_used, 3 * QT + 8 * VT // 2)
            with T.loop(4, ready_hi_ready=4) as i:
                for _ in range(4):
                    split()
            for t in range(ST):
                nc.vector.tensor_scalar(minus_sink[:, t, :], sink[:], -1.0, None, ALU.mult)
            dve.wait_ge(mask_ready, 2)
            HEADS4 = dict(ready_scores_done=4, free_p_transposed=4, ready_s_read=4, ready_p_done=4, ready_o_ready=4)
            mod_columns((SH2,))

            def panel(p, start, before, out, acc=None):
                for slot in range(SLOTS):
                    split()
                    if acc is not None:
                        ada_piece(acc, p, slot, 0)
                    elif slot == SLOTS - 1:
                        out(p)
                    heads(slot, start, before)
                if acc is not None:
                    out(p)

            def qs_out(p):
                copy_out(lambda s: QS[:, s, ds(p * PANEL, PANEL)])

            panel(0, ("mla", 0), None, qs_out)
            with T.loop(3, **DP, **HEADS4, ready_dve_step=8) as i:
                panel(i + 1, ("mla", i + 1), ("mla", i), qs_out)

            def QO(s, p):
                return Q[:, s, ds(p * (4 * (HD + ROPE)), 4 * (HD + ROPE))].rearrange("p (h n) -> p h n", h=4)[:, :, 0:HD]

            def gate_mla(p):
                for s in range(ST):
                    gated(s)
                    o = QO(s, p)
                    last = nc.vector.tensor_tensor(o, o, GATES[1][:, s, :].rearrange("p (h n) -> p h n", h=4), ALU.mult)
                last.then_inc(gates_used, 1)

            for s in range(ST):
                T.skip(acc_free[s], 4 + 4 + 6 + 8 + 4)
            dve.wait_ge(acc_zeroed, 4)
            panel(0, ("swa", 0), ("mla", 3), gate_mla, ADA_GT1)
            with T.loop(3, **OUTP, **HEADS4, ready_bias_landed0=32, ready_bias_landed1=32, ready_bias_used=4,
                        ready_acc_free0=1, ready_acc_free1=1, ready_dve_step=8) as i:
                panel(i + 1, ("swa", i + 1), ("swa", i), gate_mla, ADA_GT1)
            dve.wait_ge(acc_zeroed, 4)

            def gate_swa(p):
                for s in range(ST):
                    gated(s)
                    o = QS[:, s, ds(p * PANEL, PANEL)]
                    link(nc.vector.tensor_tensor(o, o, GATES[1][:, s, :], ALU.mult))
                    o = o.rearrange("p (h n) -> p h n", h=4)
                    last = nc.vector.tensor_tensor(o, o, QO(s, p), ALU.add)
                last.then_inc(gates_used, 1)

            def gates_panel(p, before=None):
                for slot in range(SLOTS):
                    split()
                    ada_piece(ADA_GT1, p, slot, 8)
                    heads(slot, None, before)
                gate_swa(p)

            gates_panel(0, ("swa", 3))
            with T.loop(3, **OUTP, ready_acc_free0=1, ready_acc_free1=1, ready_dve_step=2) as i:
                gates_panel(i + 1)
            dve.wait_ge(gates_used, credits["gates_used"] + 4 + 4 + 4)
            nc.vector.nop().then_inc(rows_ready, 2)
            def o_slot(slot):
                ada_piece(ADA_SH2[1], 0, slot, 8)
                if slot in (3, 6):
                    half = slot // 6
                    cols = slice(1024 * half, 1024 * (half + 1))
                    dve.wait_ge(spread_done, half + 1)
                    dve.wait_ge(row_landed, 32)
                    nc.vector.tensor_tensor(B_MIX[:, cols], PS[:, B_G:B_G + 2, :].rearrange("p b n -> p (b n)"),
                                            B_MIX[:, cols], ALU.add).then_inc(g_read, 1)
                    dve.wait_ge(g_read, half + 1)
                    link(nc.vector.tensor_tensor(G_MIX[:, cols], B_MIX[:, cols], G_MIX[:, cols], ALU.mult))

            def o_out(i):
                for s in range(ST):
                    gated(s, squares=True)
                    nc.vector.tensor_tensor(MIX[:, s, ds(i * PANEL, PANEL)], PS[:, s, :], G_MIX[:, ds(i * PANEL, PANEL)],
                                            ALU.mult).then_inc(acc_free[s], 1)

            dve.wait_ge(acc_zeroed, 5)
            first_panel(o_slot, aT_lo, aT_hi)
            o_out(0)
            with T.loop(3, **OUTP, ready_gate_ready=2) as i:
                for slot in range(SLOTS):
                    split()
                    ada_piece(ADA_SH2[1], i + 1, slot, 8)
                o_out(i + 1)
            mean(0, [D], 4)
            inverse_rms(0)
            for s in range(ST):
                dve.wait_ge(acc_free[s], 1 + N_PANELS)
            dve.wait_ge(x_again, 64)
            for j in range(2 * ST):
                s, cols = j // 2, slice(1024 * (j % 2), 1024 * (j % 2 + 1))
                nc.vector.scalar_tensor_tensor(out=X[:, s, cols], in0=MIX[:, s, cols], scalar=stat[:, 8 + s:9 + s],
                                               in1=X[:, s, cols], op0=ALU.mult, op1=ALU.add).then_inc(x2_ready, 1)
            mod_columns((SH2,), more=True)
            mean(2, [D], 2)
            inverse_rms(2)
            diagonals(2)

            def taps(pair, b, bank):
                dve.wait_ge(conv_a, T.ready(conv_a))
                for tap, shift in ((1, 1), (0, 2)):
                    for k, (dst, tile) in enumerate(((conv_g[b], pair), (conv_u[b], pair + FT))):
                        last = nc.vector.scalar_tensor_tensor(
                            out=dst[:, shift:SEQ], in0=PS[:, bank + 2 * k, 0:SEQ - shift],
                            scalar=col[:, ds(tile + (C_CONVW + P * tap), 1)], in1=dst[:, shift:SEQ],
                            op0=ALU.mult, op1=ALU.add)
                    if tap:
                        link(last)
                last.then_inc(conv_d, 1)

            def product(pair, b):
                dve.wait_ge(conv_s, T.ready(conv_s))
                nc.vector.tensor_tensor(YT[:, ds(pair, 1), :].rearrange("p a t -> p (a t)"), conv_g[b], conv_u[b],
                                        ALU.mult).then_inc(y_done, 1)

            def up_panel(before, odd, kt=None):
                for slot in range(SLOTS):
                    split()
                    if slot in (1, 2):
                        taps(before + (slot - 1), slot - 1, (0 if odd else B_UP1) + slot - 1)
                    if slot in (4, 5):
                        product(before + (slot - 4), slot - 4)
                    if slot in (0, 6) and kt is not None:
                        ada(ADA_GT2, slot // 6, kt)

            first_panel(lambda slot: None, aT_lo, aT_hi, lambda k: gains[:, 1, k:k + 1], lambda k: mod[:, SH2, k:k + 1],
                        banks=B_UP1)
            dve.wait_ge(ffn_row_landed, 32)
            UP = dict(ready_hi_ready=16, ready_conv_a=4, ready_dve_step=4, ready_conv_s=4)
            with T.loop(8, **UP, ready_ada_landed0=32, ready_ada_landed1=32, ready_ada_done=4) as i:
                up_panel(i * 4, True, i * 2)
                up_panel(i * 4 + 2, False, i * 2 + 1)
            with T.loop(2, **UP) as i:
                up_panel(i * 4 + 32, True)
                up_panel(i * 4 + 34, False)
            up_panel(40, True)
            for b in range(2):
                taps(42 + b, b, B_UP1 + b)
            for b in range(2):
                product(42 + b, b)

            def y_split(kt, slot):
                dve.wait_ge(y_hi, T.ready(y_hi))
                nc.vector.tensor_tensor(aT_lo[:, slot, :], YT[:, ds(kt, 1), :].rearrange("p a t -> p (a t)"),
                                        aT_hi[:, slot, :].bitcast(F32), ALU.subtract).then_inc(y_ready, 1)

            dve.wait_ge(y_done, credits["y_done"] + FT - 2)
            y_split(0, 0)
            dve.wait_ge(y_done, credits["y_done"] + FT)
            dve.wait_ge(g_copied, 1)
            nc.vector.tensor_tensor(G_FFN, ADA_GT2, G_FFN, ALU.mult)
            with T.loop(FT // 2 - 1, ready_hi_ready=4, ready_y_hi=2) as i:
                for j in range(2):
                    split()
                    y_split(i * 2 + (j + 1), (j + 1) % 2)
                    split()
            split()
            y_split(FT - 1, 1)
            for s in range(ST):
                dve.wait_ge(var_ready, T.ready(var_ready))
                v = stat[:, s:s + 1]
                nc.vector.tensor_scalar(v, v, 1.0 / D, EPS, ALU.mult, ALU.add).then_inc(std_ready, 1)
                inverse_rms(s, 1)
                for half in range(2):
                    cols = slice(1024 * half, 1024 * (half + 1))
                    nc.vector.scalar_tensor_tensor(
                        out=H_FFN[:, s, cols],
                        in0=PS[:, 4 * s + 2 * half:4 * s + 2 * half + 2, :].rearrange("p b n -> p (b n)"),
                        scalar=stat[:, 8 + s:9 + s], in1=G_FFN[:, cols], op0=ALU.mult, op1=ALU.mult)\
                        .then_inc(y_scaled, 1)
            dve.wait_ge(y_scaled, 2 * ST)
            nc.vector.tensor_tensor(X[:, 1, 1024:], X[:, 1, 1024:], H_FFN[:, 1, 1024:], ALU.add).then_inc(last_ready, 1)

        @block.tensor
        def _(pe):
            T = Tally(pe, credits)
            n = [0]
            give(pe, "chunk_used", "qk_transposed", "scores_done", "p_transposed", "o_ready", "sb_transposed",
                 "sb_zdone", "sb_cum", "sb_o_ready")

            def three(dst, a_hi, a_lo, w_h, w_l, first, last, weights_first=False):
                if weights_first:
                    passes = ((w_h, a_hi), (w_h, a_lo), (w_l, a_hi))
                else:
                    passes = ((a_hi, w_h), (a_hi, w_l), (a_lo, w_h))
                for j, (l, r) in enumerate(passes):
                    mm = pe.matmul(dst, l, r, start=first and j == 0, stop=last and j == 2)
                return mm

            def chunk(slot, kts, a_hi=None, a_lo=None, width=PANEL, k0=0):
                a_hi, a_lo = a_hi or aT_hi, a_lo or aT_lo
                m = n[0] % RING
                n[0] += 1
                pe.wait_ge(lo_ready, T.ready(lo_ready))
                wh = w_hi[:, m, :].rearrange("p (k n) -> p k n", k=2)
                wl = w_lo[:, m, :].rearrange("p (k n) -> p k n", k=2)
                for s in range(ST):
                    if slot == 0:
                        pe.wait_ge(acc_free[s], T.free(acc_free[s]))
                    for k in range(2):
                        kt = 2 * slot + k
                        mm = three(PS[:, s, 0:width], a_hi[:, k0 + kt, s * P:(s + 1) * P], a_lo[:, k0 + kt, s * P:(s + 1) * P],
                                   wh[:, k, 0:width], wl[:, k, 0:width], kt == 0, kt == kts - 1)
                    if slot == kts // 2 - 1 and s == 0:
                        mm.then_inc(acc_ready, 1)
                mm.then_inc(chunk_used, 1)

            def transpose_group(j, src, scale=None, banks=B_T):
                for k in range(2):
                    for s in range(ST):
                        dst = PS[:, banks + j % 4, SEQ * k + P * s:SEQ * k + P * (s + 1)]
                        if scale is None:
                            tr = pe.transpose(dst, src(s, 2 * j + k), ident[:])
                        else:
                            tr = pe.matmul(dst, src(s, 2 * j + k), diag[:, scale(2 * j + k) + s, :], start=True,
                                           stop=True)
                tr.then_inc(rows_T, 1)

            def first_panel(src, scale=None, banks=B_T, step=None, need=lambda slot: slot + 1):
                step = step or (lambda slot: chunk(slot, KT))
                pe.wait_ge(rows_ready, T.ready(rows_ready, 2))
                base = T.ready(aT_ready, 8) - 8
                for j in range(4):
                    transpose_group(j, src, scale, banks)
                for slot in range(SLOTS):
                    pe.wait_ge(aT_ready, base + need(slot))
                    step(slot)
                    if slot < 4:
                        transpose_group(slot + 4, src, scale, banks)

            def spread(acc, bank, parts):
                for b, part in enumerate(parts):
                    mm = pe.matmul(PS[:, bank + b, :], ones[:], acc[:, PANEL * part:PANEL * (part + 1)], start=True,
                                   stop=True)
                mm.then_inc(spread_done, 1)

            def ada_reduce(acc, parts=1):
                for k in range(parts * KT):
                    mm = pe.matmul(PS[:, B_O, k:k + 1], acc[:, P * k:P * (k + 1)], ones[:, 0:1], start=True, stop=True)
                mm.then_inc(ada_cols, 1)

            def head_T(kind, j=0):
                pe.wait_ge(stage_full, T.ready(stage_full))
                pe.wait_ge(qkT_full, T.free(qkT_full))
                for qk in range(1 if kind == "swa" and j else 2):
                    for s in range(ST):
                        tr = pe.transpose(PS[:, B_T, SEQ * qk + P * s:SEQ * qk + P * (s + 1)], stage[:, s, qk, :], ident[:])
                if kind == "mla":
                    for s in range(ST):
                        tr = pe.transpose(PS[0:ROPE, B_S1, P * s:P * (s + 1)], stage_r[:, s, :], ident[:])
                tr.then_inc(qk_transposed, 1)

            def head_S(kind):
                pe.wait_ge(qkT_full, T.ready(qkT_full))
                pe.wait_ge(s_read, T.free(s_read))
                for e in range(2 if kind == "swa" else 1):
                    p0, p1 = (SWA_D * e, SWA_D * (e + 1)) if kind == "swa" else (0, P)
                    for t in range(ST):
                        dst = PS[:, B_S0 + e, P * t:P * t + P * (t + 1)]
                        mm = pe.matmul(dst, qkT[p0:p1, P * t:P * (t + 1)], qkT[p0:p1, SEQ:SEQ + P * (t + 1)],
                                       start=True, stop=kind != "mla")
                        if kind == "mla":
                            mm = pe.matmul(dst, qrT[:, P * t:P * (t + 1)], krT[:, 0:P * (t + 1)], start=False, stop=True)
                mm.then_inc(scores_done, 1)

            def head_P(kind):
                pe.wait_ge(p_done, T.ready(p_done))
                pe.wait_ge(pT_full, T.free(pT_full))
                for e in range(2 if kind == "swa" else 1):
                    for b in range(3):
                        tr = pe.transpose(PS[:, B_P + e, P * b:P * (b + 1)], s_sb[:, e, P * b:P * (b + 1)], ident[:])
                tr.then_inc(p_transposed, 1)

            def head_O(kind, v, heads=1, w=HD):
                pe.wait_ge(pT_full, T.ready(pT_full))
                pe.wait_ge(o_done, T.free(o_done))
                for e in range(heads):
                    pe.matmul(PS[:, B_O, w * e:w * (e + 1)], pT[:, e, 0:P], v(0), start=True, stop=True)
                    dst = PS[:, B_O, HD + w * e:HD + w * (e + 1)]
                    pe.matmul(dst, pT[:, e, P:2 * P], v(0), start=True, stop=False)
                    mm = pe.matmul(dst, pT[:, e, 2 * P:3 * P], v(1), start=False, stop=True)
                mm.then_inc(o_ready, 1)

            def sb_T():
                pe.wait_ge(sb_staged, T.ready(sb_staged))
                pe.wait_ge(sb_qkT, T.free(sb_qkT))
                for qk in range(2):
                    for s in range(ST):
                        tr = pe.transpose(PS[:, B_T, SEQ * qk + P * s:SEQ * qk + P * (s + 1)], stage[:, s, qk, :], ident[:])
                tr.then_inc(sb_transposed, 1)

            def sb_Z(b):
                pe.wait_ge(sb_qkT, T.ready(sb_qkT))
                pe.wait_ge(sb_w_done, T.free(sb_w_done))
                pe.matmul(PS[:, B_Z[b][0], 0:SEQ], qkT[:, SEQ:SEQ + P], qkT[:, 0:SEQ], start=True, stop=False,
                          skip_group_check=True)
                pe.matmul(PS[:, B_Z[b][1], 0:P], qkT[:, SEQ + P:], qkT[:, P:SEQ], start=True, stop=False,
                          skip_group_check=True).then_inc(sb_zdone, 1)

            def sb_C(b):
                pe.wait_ge(sb_spdone, T.ready(sb_spdone))
                z0, z1 = PS[:, B_Z[b][0], 0:SEQ], PS[:, B_Z[b][1], 0:P]
                on_top = dict(start=False, skip_group_check=True)
                pe.matmul(z0, tri[:], s_sb[:, 0, 0:SEQ], stop=False, **on_top)
                pe.matmul(z0[:, P:], minus1[:], s_sb[:, 1, 0:P], stop=False, **on_top)
                pe.matmul(z0[:, 0:P], ident_b[:], neg_b[:], stop=True, **on_top)
                pe.matmul(z1, tri[:], s_sb[:, 1, 0:P], stop=False, **on_top)
                pe.matmul(z1, ident_b[:], neg_b[:], stop=True, **on_top).then_inc(sb_cum, 1)

            def sb_O(h):
                pe.wait_ge(sb_w_done, T.ready(sb_w_done))
                pe.wait_ge(sb_o_done, T.free(sb_o_done))
                v = lambda s: QKV_A[:, s, ds(h * HD + 2 * N_A * HD, HD)]
                pe.matmul(PS[:, B_O, 0:HD], pT[:, 0, 0:P], v(0), start=True, stop=True)
                pe.matmul(PS[:, B_O, HD:2 * HD], pT[:, 0, P:SEQ], v(0), start=True, stop=False)
                pe.matmul(PS[:, B_O, HD:2 * HD], pT[:, 1, 0:P], v(1), start=False, stop=True).then_inc(sb_o_ready, 1)

            pe.wait_ge(const_ready, 1)
            pe.wait_ge(par_landed, 16 * 13)
            for t, r in enumerate(PARAM_ROWS):
                tr = pe.transpose(PS[:, 6 + t // 4, P * (t % 4):P * (t % 4) + r], PARAM[0:r, t, :], ident[0:r, 0:r])
            tr.then_inc(par_T, 1)
            pe.wait_ge(par_ready, 1)
            first_panel(lambda s, k: X[:, s, P * k:P * (k + 1)], lambda k: 0)
            pe.wait_ge(misc_landed, 48)
            pe.matmul(PS[0:SWA_H, B_O - 1, 0:383], table, hot, start=True, stop=True).then_inc(win_cols, 1)
            with T.loop(5, **PE_PANEL) as i:
                for slot in range(SLOTS):
                    chunk(slot, KT)
            with T.loop(4, **PE_PANEL, ready_stage_full=2, free_qkT_full=2, ready_qkT_full=2, free_s_read=2,
                        ready_p_done=2, free_pT_full=2, ready_pT_full=2, free_o_done=2) as i:
                for slot in range(SLOTS):
                    chunk(slot, KT)
                    if slot - 4 in START_B:
                        j = START_B.index(slot - 4)
                        head_O("b", lambda s: QKV_B[:, s, ds(i * (2 * HD) + (j + 2 * N_B) * HD, HD)])
                    if slot - 3 in START_B:
                        head_P("b")
                    if slot - 1 in START_B:
                        head_S("b")
                    if slot in START_B:
                        head_T("b")
            with T.loop(2, **PE_PANEL) as i:
                for slot in range(SLOTS):
                    chunk(slot, KT)
            pe.wait_ge(o_done, credits["o_done"] + N_B)

            def values(kind, i, j):
                if kind == "mla":
                    return lambda s: KV[:, s, ds(i * (8 * HD) + (2 * j + 1) * HD, HD)]
                return lambda s: KVS[:, s, ds(i * SWA_D + SWA_G * SWA_D, SWA_D)]

            def panel(start=None, before=None):
                for slot in range(SLOTS):
                    chunk(slot, KT)
                    if h := due(slot, 4, start, before):
                        if h[0] == "sb":
                            sb_O(h[1] * 4 + h[2])
                        else:
                            head_O(h[0], values(*h), *((2, SWA_D) if h[0] == "swa" else ()))
                    if h := due(slot, 3, start, before):
                        sb_C(h[2] % 2) if h[0] == "sb" else head_P(h[0])
                    if h := due(slot, 1, start, before):
                        sb_Z(h[2] % 2) if h[0] == "sb" else head_S(h[0])
                    if h := due(slot, 0, start, before):
                        sb_T() if h[0] == "sb" else head_T(h[0], h[2])

            for start, before in ((("sb", 0), None), (("sb", 1), ("sb", 0)), (None, ("sb", 1)), (None, None)):
                panel(start, before)
            pe.wait_ge(acc_free[0], 1 + 16)
            pe.wait_ge(acc_free[1], 1 + 16)
            first_panel(lambda s, k: (QKV_A if k < 8 else QKV_B)[:, s, P * (k % 8):P * (k % 8 + 1)])
            pe.wait_ge(ada_done, credits["ada_done"] + 64)
            ada_reduce(ADA_1, 2)
            with T.loop(3, **PE_PANEL) as i:
                for slot in range(SLOTS):
                    chunk(slot, KT)
            first_panel(lambda s, k: X[:, s, P * k:P * (k + 1)], lambda k: 0)
            for slot in range(SLOTS):
                chunk(slot, KT)
            for slot in range(SLOTS):
                chunk(slot, KT, width=LAT - 2 * PANEL)
            base = T.ready(aT_ready, 5) - 5
            for slot in range(SLOTS):
                chunk(slot, KT)
                if slot == 2:
                    pe.wait_ge(rows_ready, T.ready(rows_ready, 2))
                if 2 <= slot < 7:
                    if slot == 6:
                        pe.wait_ge(aT_ready, base + 1)
                    transpose_group(slot - 2, lambda s, k: LATR[:, s, P * k:P * (k + 1)], lambda k: 0 if k < QT else ST)
            pe.wait_ge(aT_ready, base + 5)
            pe.wait_ge(kr_staged, 1)
            for s in range(ST):
                tr = pe.transpose(PS[0:ROPE, B_O, P * s:P * (s + 1)], stage_r[:, s, :], ident[:])
            tr.then_inc(kr_T, 1)
            pe.wait_ge(kr_ready, 1)
            pe.wait_ge(ada_done, credits["ada_done"] + 64 + 32)
            pe.wait_ge(mod_ready, 1)
            ada_reduce(ADA_SC2)
            for c in range(3):
                for kt in range(QT):
                    m = n[0] % RING
                    n[0] += 1
                    pe.wait_ge(lo_ready, T.ready(lo_ready))
                    for half in range(2):
                        for s in range(ST):
                            if kt == 0 and half == 0:
                                pe.wait_ge(acc_free[s], T.free(acc_free[s], 2 if c else 1))
                            cols = slice(PANEL * half, PANEL * (half + 1))
                            mm = three(PS[:, 2 * half + s, :], latT_hi[:, kt, s * P:(s + 1) * P],
                                       latT_lo[:, kt, s * P:(s + 1) * P], w_hi[:, m, cols], w_lo[:, m, cols],
                                       kt == 0, kt == QT - 1)
                            if kt == QT - 1 and (half, s) != (1, 1):
                                mm.then_inc(acc_ready, 1)
                    mm.then_inc(chunk_used, 1)
            for s in range(ST):
                T.skip(acc_free[s], 1, "free")
            pe.wait_ge(ada_done, credits["ada_done"] + 64 + 32 + 16)
            pe.wait_ge(mod_ready, 3)
            ada_reduce(ADA_SH2[0])
            with T.loop(4, ready_lo_ready=4, free_acc_free0=2, free_acc_free1=2) as i:
                for j in range(2):
                    for slot in range(2):
                        chunk(slot, VT, latT_hi, latT_lo, k0=QT)
            HEADS4 = dict(ready_stage_full=4, free_qkT_full=4, ready_qkT_full=4, free_s_read=4,
                          ready_p_done=4, free_pT_full=4, ready_pT_full=4, free_o_done=4)
            panel(("mla", 0))
            with T.loop(3, **PE_PANEL, **HEADS4) as i:
                panel(("mla", i + 1), ("mla", i))
            panel(("swa", 0), ("mla", 3))
            with T.loop(3, **PE_PANEL, **HEADS4) as i:
                panel(("swa", i + 1), ("swa", i))
            panel(None, ("swa", 3))
            with T.loop(3, **PE_PANEL) as i:
                panel()

            def o_step(slot):
                chunk(slot, KT)
                if slot in (2, 5):
                    if slot == 2:
                        pe.wait_ge(ada_done, credits["ada_done"] + 64 + 32 + 16 + 32)
                    else:
                        pe.wait_ge(g_read, 1)
                    spread(ADA_GT1, B_G, (0, 1) if slot == 2 else (2, 3))

            first_panel(lambda s, k: QS[:, s, P * k:P * (k + 1)], step=o_step)
            with T.loop(3, **PE_PANEL) as i:
                for slot in range(SLOTS):
                    chunk(slot, KT)
            pe.wait_ge(ada_done, credits["ada_done"] + 64 + 96)
            ada_reduce(ADA_SH2[1])

            def up_chunk(slot, odd):
                m = n[0] % RING
                n[0] += 1
                pe.wait_ge(lo_ready, T.ready(lo_ready))
                wh = w_hi[:, m, :].rearrange("p (k n) -> p k n", k=4)
                wl = w_lo[:, m, :].rearrange("p (k n) -> p k n", k=4)
                for e in range(2):
                    if slot == 0:
                        pe.wait_ge(conv_d, T.free(conv_d))
                    for k in range(4):
                        kt = 4 * (slot // 2) + k
                        mm = three(PS[:, (B_UP1 if odd else 0) + 2 * (slot % 2) + e, 0:SEQ], aT_hi[:, kt, :], aT_lo[:, kt, :],
                                   wh[:, k, P * e:P * (e + 1)], wl[:, k, P * e:P * (e + 1)],
                                   kt == 0, kt == KT - 1, weights_first=True)
                mm.then_inc(chunk_used, 1)

            pe.wait_ge(acc_free[0], 1 + N_PANELS)
            pe.wait_ge(acc_free[1], 1 + N_PANELS)
            first_panel(lambda s, k: X[:, s, P * k:P * (k + 1)], lambda k: 0, B_UP1, lambda slot: up_chunk(slot, False),
                        lambda slot: 2 * (slot // 2) + 2)
            with T.loop(10, ready_lo_ready=16, free_conv_d=4) as i:
                for odd in (True, False):
                    for slot in range(SLOTS):
                        up_chunk(slot, odd)
            for slot in range(SLOTS):
                up_chunk(slot, True)
            pe.wait_ge(ada_done, credits["ada_done"] + 64 + 96 + 32)
            pe.wait_ge(conv_d, credits["conv_d"] + FT - 2)
            spread(ADA_GT2, 0, range(4))
            pe.wait_ge(g_copied, 1)
            def down(j, first=False, last=False):
                pe.wait_ge(y_ready, T.ready(y_ready))
                at = [(n[0] + half) % RING for half in range(2)]
                n[0] += 2
                for s in range(ST):
                    if first and s == 1:
                        pe.wait_ge(conv_d, credits["conv_d"] + FT)
                    for half in range(2):
                        if s == 0:
                            pe.wait_ge(lo_ready, T.ready(lo_ready))
                        for c in range(2):
                            cols = slice(PANEL * c, PANEL * (c + 1))
                            mm = three(PS[:, 4 * s + 2 * half + c, :], aT_hi[:, j, s * P:(s + 1) * P],
                                       aT_lo[:, j, s * P:(s + 1) * P], w_hi[:, at[half], cols], w_lo[:, at[half], cols],
                                       first, last)
                        if s == ST - 1 and not last:
                            mm.then_inc(chunk_used, 1)
                    if last:
                        mm.then_inc(down_done, 1)

            down(0, first=True)
            with T.loop(FT // 2 - 1, ready_y_ready=2, ready_lo_ready=4) as i:
                for j in range(2):
                    down((j + 1) % 2)
            down(1, last=True)


_INS = ["x", "norm_g", "w_in", "q_norm_g", "k_norm_g", "rel_bias", "w_out", "c_2", "w_ada_2", "b_ada_2", "g_pre_mix_2",
        "g_post_mix_2", "w_in_2", "g_q_lat_2", "w_uq_2", "g_kv_lat_2", "w_ukv_2", "rel_bias_2", "sinks_2", "w_o_2",
        "g_pre_ffn_2", "g_post_ffn_2", "w_up_2", "conv_w_2", "conv_b_2", "w_down_2",
        "rope_cos", "rope_sin", "bucket_hot"]


def rope_tables():
    inv = (np.float32(10000.0) ** (-np.arange(0, ROPE, 2, dtype=np.float32) / np.float32(ROPE))).astype(np.float32)
    angle = np.arange(SEQ, dtype=np.float32)[:, None] * inv[None, :]
    cos, sin = np.cos(angle).astype(np.float32), np.sin(angle).astype(np.float32)
    return np.concatenate([cos, cos], 1), np.concatenate([-sin, sin], 1)


def bucket_rows():
    hot = np.zeros((BUCKETS + 1, 383), np.float32)
    exact = BUCKETS // 2
    for m in range(383):
        dist = m - (P - 1)
        if not 0 <= dist < WINDOW:
            hot[BUCKETS, m] = 1.0
            continue
        bucket = dist
        if dist >= exact:
            bucket = exact + int(np.log(np.float32(dist) / np.float32(exact)) / np.float32(np.log(WINDOW / exact))
                                 * np.float32(BUCKETS - exact))
        hot[min(bucket, BUCKETS - 1), m] = 1.0
    return hot


def kernel(**inputs):
    import concourse.bacc as bacc
    from concourse.bass_utils import run_bass_kernel_spmd

    arrays = {k: np.ascontiguousarray(v) for k, v in inputs.items()}
    arrays["rope_cos"], arrays["rope_sin"] = rope_tables()
    arrays["bucket_hot"] = bucket_rows()
    nc = bacc.Bacc("TRN2", target_bir_lowering=False, num_devices=1)
    args = [nc.dram_tensor(f"in_{n}", arrays[n].shape, mybir.dt.from_np(arrays[n].dtype), kind="ExternalInput").ap()
            for n in _INS]
    args.append(nc.dram_tensor("out_rows", (1, SEQ, D), F32, kind="ExternalOutput").ap())
    block_kernel(nc, *args)
    r = run_bass_kernel_spmd(nc, [{f"in_{n}": arrays[n] for n in _INS}], core_ids=[0])
    return r.results[0]["out_rows"]
```
